# Optimizing a Trainium2 kernel written in Bass

```python
import jax, jax.numpy as jnp
from jax import lax
import numpy as np

D_MODEL = 1024
BATCH = 1
SEQ = 256
DEPTH = 2

CHUNK = 64
Q_BLOCK = 128
N_A_LAYERS = max(1, DEPTH // 2)
N_B_LAYERS = DEPTH - N_A_LAYERS
N_DENSE = (DEPTH + 1) // 2
N_MOE = DEPTH // 2

MLA_HEADS = 16
MLA_NOPE = 64
MLA_ROPE = 32
MLA_QK = MLA_NOPE + MLA_ROPE
MLA_V = 64
Q_LORA = 384
KV_LORA = 256
ROPE_THETA = 10000.0

CA_HEADS = 16
CA_HEAD_DIM = D_MODEL // CA_HEADS
LEFT_CHUNKS = 8
BAND = (LEFT_CHUNKS + 1) * CHUNK
REL_CLIP = 128

DENSE_FF = 2816
N_EXPERTS = 8
TOP_K = 2
EXPERT_FF = 3584

EPS = 1e-6

kernel_name = "yoco_mla_chunkband_moe_trunk"

def rms_norm(x, g):
    xf = x.astype(jnp.float32)
    y = xf * lax.rsqrt(jnp.mean(xf * xf, axis=-1, keepdims=True) + EPS)
    return (y * g.astype(jnp.float32)).astype(x.dtype)

def rope(x, pos):
    half = x.shape[-1] // 2
    inv = ROPE_THETA ** (-jnp.arange(half, dtype=jnp.float32) / half)
    ang = pos.astype(jnp.float32)[:, None] * inv[None, :]
    cos = jnp.cos(ang)[:, None, :]
    sin = jnp.sin(ang)[:, None, :]
    xf = x.astype(jnp.float32)
    x1, x2 = xf[..., :half], xf[..., half:]
    return jnp.concatenate([x1 * cos - x2 * sin, x2 * cos + x1 * sin], axis=-1).astype(x.dtype)

def swiglu(h, w1, w3, w2):
    return (jax.nn.silu(h @ w1) * (h @ w3)) @ w2

def block_causal_attention(q, k, v, scale):
    B, S, H, Dq = q.shape
    Dv = v.shape[-1]
    nb = S // Q_BLOCK
    qb = q.reshape(B, nb, Q_BLOCK, H, Dq).transpose(1, 0, 2, 3, 4)
    kchunk = jnp.arange(S) // CHUNK
    neg = jnp.finfo(jnp.float32).min

    def one(args):
        qblk, ib = args
        s = jnp.einsum('bqhd,bkhd->bhqk', qblk, k).astype(jnp.float32) * scale
        qchunk = (ib * Q_BLOCK + jnp.arange(Q_BLOCK)) // CHUNK
        mask = kchunk[None, :] <= qchunk[:, None]
        s = jnp.where(mask[None, None], s, neg)
        p = jax.nn.softmax(s, axis=-1).astype(v.dtype)
        return jnp.einsum('bhqk,bkhd->bqhd', p, v)

    o = lax.map(one, (qb, jnp.arange(nb)))
    return o.transpose(1, 0, 2, 3, 4).reshape(B, S, H, Dv)

def mla_attention(h, w_dq, g_cq, w_uq, w_dkv, g_ckv, w_ukv, g_qn, g_kn, w_o):
    B, S, _ = h.shape
    pos = jnp.arange(S)
    c_q = rms_norm(h @ w_dq, g_cq)
    q = (c_q @ w_uq).reshape(B, S, MLA_HEADS, MLA_QK)
    kv_a = h @ w_dkv
    c_kv = rms_norm(kv_a[..., :KV_LORA], g_ckv)
    k_pe = jnp.broadcast_to(kv_a[:, :, None, KV_LORA:], (B, S, MLA_HEADS, MLA_ROPE))
    kv = (c_kv @ w_ukv).reshape(B, S, MLA_HEADS, MLA_NOPE + MLA_V)
    k_nope, v = kv[..., :MLA_NOPE], kv[..., MLA_NOPE:]
    k = jnp.concatenate([k_nope, k_pe], axis=-1)
    q = rms_norm(q, g_qn)
    k = rms_norm(k, g_kn)
    q = jnp.concatenate([q[..., :MLA_NOPE], rope(q[..., MLA_NOPE:], pos)], axis=-1)
    k = jnp.concatenate([k[..., :MLA_NOPE], rope(k[..., MLA_NOPE:], pos)], axis=-1)
    o = block_causal_attention(q, k, v, MLA_QK ** -0.5)
    return o.reshape(B, S, MLA_HEADS * MLA_V) @ w_o

def shared_band_kv(x, g_kv, w_k, w_v, g_kn):
    B, S, _ = x.shape
    h = rms_norm(x, g_kv)
    k = rms_norm((h @ w_k).reshape(B, S, CA_HEADS, CA_HEAD_DIM), g_kn)
    v = (h @ w_v).reshape(B, S, CA_HEADS, CA_HEAD_DIM)
    pad = ((0, 0), (LEFT_CHUNKS * CHUNK, 0), (0, 0), (0, 0))
    return jnp.pad(k, pad), jnp.pad(v, pad)

def chunked_band_attention(h, w_q, g_qn, rel_bias, w_o, k_pad, v_pad):
    B, S, _ = h.shape
    nc = S // CHUNK
    q = rms_norm((h @ w_q).reshape(B, S, CA_HEADS, CA_HEAD_DIM), g_qn)
    i = jnp.arange(CHUNK)
    j = jnp.arange(BAND)
    rel = i[:, None] + LEFT_CHUNKS * CHUNK - j[None, :]
    idx = jnp.clip(rel, -REL_CLIP, REL_CLIP) + REL_CLIP
    bias = rel_bias[:, idx].astype(jnp.float32)
    qc = q.reshape(B, nc, CHUNK, CA_HEADS, CA_HEAD_DIM).transpose(1, 0, 2, 3, 4)
    neg = jnp.finfo(jnp.float32).min
    scale = CA_HEAD_DIM ** -0.5

    def one(args):
        qch, c = args
        kb = lax.dynamic_slice_in_dim(k_pad, c * CHUNK, BAND, axis=1)
        vb = lax.dynamic_slice_in_dim(v_pad, c * CHUNK, BAND, axis=1)
        s = jnp.einsum('bqhd,bkhd->bhqk', qch, kb).astype(jnp.float32) * scale + bias[None]
        valid = (c - LEFT_CHUNKS) * CHUNK + j >= 0
        s = jnp.where(valid[None, None, None, :], s, neg)
        p = jax.nn.softmax(s, axis=-1).astype(vb.dtype)
        return jnp.einsum('bhqk,bkhd->bqhd', p, vb)

    o = lax.map(one, (qc, jnp.arange(nc)))
    o = o.transpose(1, 0, 2, 3, 4).reshape(B, S, CA_HEADS * CA_HEAD_DIM)
    return o @ w_o

def moe_swiglu(h, w_router, w1, w3, w2):
    B, S, D = h.shape
    t = h.reshape(B * S, D)
    logits = (t @ w_router).astype(jnp.float32)
    top_vals, top_idx = lax.top_k(logits, TOP_K)
    gates = jax.nn.softmax(top_vals, axis=-1)
    combine = jnp.sum(jax.nn.one_hot(top_idx, N_EXPERTS, dtype=jnp.float32) * gates[..., None], axis=1)
    y = jnp.zeros_like(t)
    for e in range(N_EXPERTS):
        y = y + combine[:, e:e + 1].astype(t.dtype) * swiglu(t, w1[e], w3[e], w2[e])
    return y.reshape(B, S, D)

def setup_inputs(seed: int = 0) -> dict:
    key = jax.random.key(seed)
    ks = list(jax.random.split(key, 32))
    f32 = jnp.float32

    def w(k, shape, fan_in):
        return jax.random.normal(k, shape, f32) * (fan_in ** -0.5)

    def gain(k, shape):
        return 1.0 + 0.02 * jax.random.normal(k, shape, f32)

    D = D_MODEL
    return {
        "x": jax.random.normal(ks[0], (BATCH, SEQ, D), f32),
        "attn_norm": gain(ks[1], (DEPTH, D)),
        "ffn_norm": gain(ks[2], (DEPTH, D)),
        "a_w_dq": w(ks[3], (N_A_LAYERS, D, Q_LORA), D),
        "a_g_cq": gain(ks[4], (N_A_LAYERS, Q_LORA)),
        "a_w_uq": w(ks[5], (N_A_LAYERS, Q_LORA, MLA_HEADS * MLA_QK), Q_LORA),
        "a_w_dkv": w(ks[6], (N_A_LAYERS, D, KV_LORA + MLA_ROPE), D),
        "a_g_ckv": gain(ks[7], (N_A_LAYERS, KV_LORA)),
        "a_w_ukv": w(ks[8], (N_A_LAYERS, KV_LORA, MLA_HEADS * (MLA_NOPE + MLA_V)), KV_LORA),
        "a_g_qn": gain(ks[9], (N_A_LAYERS, MLA_QK)),
        "a_g_kn": gain(ks[10], (N_A_LAYERS, MLA_QK)),
        "a_w_o": w(ks[11], (N_A_LAYERS, MLA_HEADS * MLA_V, D), MLA_HEADS * MLA_V),
        "kv_norm": gain(ks[12], (D,)),
        "kv_w_k": w(ks[13], (D, CA_HEADS * CA_HEAD_DIM), D),
        "kv_w_v": w(ks[14], (D, CA_HEADS * CA_HEAD_DIM), D),
        "kv_g_kn": gain(ks[15], (CA_HEAD_DIM,)),
        "b_w_q": w(ks[16], (N_B_LAYERS, D, CA_HEADS * CA_HEAD_DIM), D),
        "b_g_qn": gain(ks[17], (N_B_LAYERS, CA_HEAD_DIM)),
        "b_rel_bias": 0.1 * jax.random.normal(ks[18], (N_B_LAYERS, CA_HEADS, 2 * REL_CLIP + 1), f32),
        "b_w_o": w(ks[19], (N_B_LAYERS, CA_HEADS * CA_HEAD_DIM, D), CA_HEADS * CA_HEAD_DIM),
        "ffn_w1": w(ks[20], (N_DENSE, D, DENSE_FF), D),
        "ffn_w3": w(ks[21], (N_DENSE, D, DENSE_FF), D),
        "ffn_w2": w(ks[22], (N_DENSE, DENSE_FF, D), DENSE_FF),
        "moe_router": w(ks[23], (N_MOE, D, N_EXPERTS), D),
        "moe_w1": w(ks[24], (N_MOE, N_EXPERTS, D, EXPERT_FF), D),
        "moe_w3": w(ks[25], (N_MOE, N_EXPERTS, D, EXPERT_FF), D),
        "moe_w2": w(ks[26], (N_MOE, N_EXPERTS, EXPERT_FF, D), EXPERT_FF),
    }

def reference(x, attn_norm, ffn_norm, a_w_dq, a_g_cq, a_w_uq, a_w_dkv, a_g_ckv, a_w_ukv,
              a_g_qn, a_g_kn, a_w_o, kv_norm, kv_w_k, kv_w_v, kv_g_kn, b_w_q, b_g_qn,
              b_rel_bias, b_w_o, ffn_w1, ffn_w3, ffn_w2, moe_router, moe_w1, moe_w3, moe_w2):
    k_pad = None
    v_pad = None
    for layer in range(DEPTH):
        h = rms_norm(x, attn_norm[layer])
        if layer < N_A_LAYERS:
            la = layer
            x = x + mla_attention(h, a_w_dq[la], a_g_cq[la], a_w_uq[la], a_w_dkv[la], a_g_ckv[la],
                                  a_w_ukv[la], a_g_qn[la], a_g_kn[la], a_w_o[la])
        else:
            lb = layer - N_A_LAYERS
            x = x + chunked_band_attention(h, b_w_q[lb], b_g_qn[lb], b_rel_bias[lb], b_w_o[lb],
                                           k_pad, v_pad)
        h = rms_norm(x, ffn_norm[layer])
        if layer % 2 == 0:
            ld = layer // 2
            x = x + swiglu(h, ffn_w1[ld], ffn_w3[ld], ffn_w2[ld])
        else:
            lm = layer // 2
            x = x + moe_swiglu(h, moe_router[lm], moe_w1[lm], moe_w3[lm], moe_w2[lm])
        if layer == N_A_LAYERS - 1:
            k_pad, v_pad = shared_band_kv(x, kv_norm, kv_w_k, kv_w_v, kv_g_kn)
    return x


_drawn_inputs = setup_inputs


def setup_inputs(seed=0):
    import zlib

    import numpy as np

    out = dict(_drawn_inputs(seed))
    spreads = {}
    factors = {'attn_norm': 5.955,
     'a_g_cq': 8.0,
     'a_g_ckv': 6.792,
     'a_g_qn': 4.385,
     'a_g_kn': 3.912,
     'kv_norm': 8.0,
     'kv_g_kn': 8.0,
     'b_g_qn': 8.0,
     'b_rel_bias': 5.522}
    for name, (base, spread) in spreads.items():
        noise = np.random.default_rng([zlib.crc32(name.encode()), seed]).standard_normal(out[name].shape)
        drawn = base * np.exp(spread * noise) if base else spread * noise
        out[name] = __import__('jax').numpy.asarray(drawn.astype(out[name].dtype))
    for name, factor in factors.items():
        out[name] = (out[name] * factor).astype(out[name].dtype)
    return out
```

```python
import concourse.bass as bass
from concourse import mybir
from contextlib import ExitStack

P = 128
D = 1024
SEQ = 256
T = SEQ // P
DC = D // P
CHUNK = 64
HEADS = 16
PAIRS = HEADS // 2
NOPE, ROPE, VDIM = 64, 32, 64
QK = NOPE + ROPE
HALF = ROPE // 2
Q_LORA, KV_LORA = 384, 256
QC, KVC = Q_LORA // P, KV_LORA // P
HD = D // HEADS
FF = 2816
FW = 256
FSTEPS = FF // FW
NE = 8
EFF = 3584
EW = 512
ESTEPS = EFF // EW
EPS = 1e-6
SPAN = P + SEQ
UNIT = 2048
RAW = 6
SPLIT = 3

U_DQ, U_DKV, U_UQ, U_UKV, U_WO0 = 0, 2, 4, 7, 9
U_FFN = 13
U_L1 = U_FFN + 3 * FSTEPS
U_MOE = U_L1 + 16
U_RUN = 6 * ESTEPS
V_EXTRA = 3

C_ID, C_TRI, C_IOTA, C_ONES, C_ROPC, C_ROPS, C_REV, C_MA, C_MB = 0, 128, 256, 384, 512, 576, 640, 656, 784
C_ALL = C_MB + CHUNK
MASKED = -1e30

G_ATT, G_FFN, G_KV, G_CQ, G_CKV = 0, 16, 32, 40, 43
G_ALL = 45


def width(n):
    if n < U_DKV:
        return 4 * Q_LORA
    if n < U_UQ:
        return 4 * (KV_LORA + ROPE)
    if n < U_UKV:
        return QC * 512
    return UNIT


def trunk_kernel(nc, x, attn_norm, ffn_norm, w_dq, g_cq, w_uq, w_dkv, g_ckv, w_ukv, g_qn, g_kn, w_oa,
                 kv_norm, w_k, w_v, g_kk, w_q, g_qq, bias_rows, w_ob, w1, w3, w2, router, mw1, mw3, mw2,
                 consts, out):
    fp32, f32r, i32 = mybir.dt.float32, mybir.dt.float32r, mybir.dt.int32
    ALU = mybir.AluOpType
    ACT = mybir.ActivationFunctionType
    AX = mybir.AxisListType.X
    ds = bass.ds

    bias_wide = nc.dram_tensor("bias_wide", (HEADS, P, SPAN), fp32, kind="Internal").ap()

    x_v = x.rearrange("b (t p) d -> p (b t) d", p=P)
    out_v = out.rearrange("b (t p) d -> p (b t) d", p=P)

    def rows(w):
        return w.rearrange("(c p) n -> p c n", p=P)

    dq_v, uq_v, dkv_v, ukv_v, oa_v = (rows(w.rearrange("a d n -> (a d) n")) for w in (w_dq, w_uq, w_dkv, w_ukv, w_oa))
    l1_v = [rows(w_q.rearrange("a d n -> (a d) n")), rows(w_k), rows(w_v), rows(w_ob.rearrange("a d n -> (a d) n"))]
    w1_v, w3_v, w2_v = (rows(w.rearrange("a d n -> (a d) n")) for w in (w1, w3, w2))
    m1_v, m3_v, m2_v = (rows(w.rearrange("a e d n -> (a e d) n")) for w in (mw1, mw3, mw2))
    rt_v = rows(router.rearrange("a d n -> (a d) n"))

    ctx = ExitStack()
    with ctx:
        def sem(name):
            return ctx.enter_context(nc.semaphore(name))

        def sb(name, shape, dt=fp32, at=ctx):
            return at.enter_context(nc.sbuf_tensor(name, shape, dt))

        xr = sb("xr", [P, T, D])
        tn = sb("tn", [P, T, D])
        hth = sb("hth", [P, DC, SEQ], f32r)
        htl = sb("htl", [P, DC, SEQ], f32r)
        raw = sb("raw", [P, RAW, UNIT])
        wh_a = sb("wh_a", [P, SPLIT, UNIT], f32r)
        wl_a = sb("wl_a", [P, SPLIT, UNIT], f32r)
        cst = sb("cst", [P, C_ALL])
        grow = sb("grow", [G_ALL, P])
        gcol = sb("gcol", [P, G_ALL])
        qkg = sb("qkg", [P, 2, 2])
        pe_g = sb("pe_g", [P, 2, 2, ROPE])
        ropt = sb("ropt", [P, 2, 2, T, ROPE])
        negh = sb("negh", [P, 2 * T * HEADS])
        ss = sb("ss", [P, 4])
        rstd = sb("rstd", [P, 4])
        ssh = sb("ssh", [P, 2, T, HEADS])
        rsh = sb("rsh", [P, 2, T, HEADS])
        nmax = sb("nmax", [P, 2, T, 2])
        rsum = sb("rsum", [P, 2, T, 2])
        rinv = sb("rinv", [P, 2, T, 2])
        wr = sb("wr", [P, DC, NE])
        wrh = sb("wrh", [P, DC, NE], f32r)
        wrl = sb("wrl", [P, DC, NE], f32r)

        lg = sb("lg", [P, T, NE])
        work = sb("work", [P, 8, T, NE])
        tops = sb("tops", [P, 8, T])
        over = sb("over", [P, 4, NE])
        pos_v = sb("pos_v", [P, NE + V_EXTRA + 1, T])
        gate_v = sb("gate_v", [P, NE + V_EXTRA + 1, T])
        tabf = sb("tabf", [P, 8])
        tab = sb("tab", [P, 8], i32)
        kpr = sb("kpr", [P, T, ROPE])

        pre = ExitStack()
        q_all = sb("q_all", [P, T, HEADS * QK], at=pre)
        kv_all = sb("kv_all", [P, T, 2 * D], at=pre)
        att = ExitStack()
        qn = sb("qn", [P, 2, T, 2 * QK], at=att)
        kn = sb("kn", [P, 2, T, 2 * QK], at=att)
        qT = sb("qT", [P, 2, 2 * SEQ], at=att)
        kT = sb("kT", [P, 2, 2 * SEQ], at=att)
        prob = sb("prob", [P, 2, 2, SPAN], at=att)
        probT = sb("probT", [P, 2, 2, SPAN], at=att)
        bias = sb("bias", [P, 2, 2, SPAN], at=att)
        att.close()
        sq = ExitStack()
        squares = sb("squares", [P, T * HEADS * QK], at=sq)
        roptmp = sb("roptmp", [P, 2, HEADS, ROPE], at=sq)
        kpe = sb("kpe", [P, T, ROPE], at=sq)
        ch = sb("ch", [P, QC + KVC, SEQ], f32r, at=sq)
        cl = sb("cl", [P, QC + KVC, SEQ], f32r, at=sq)
        sq.close()
        l1 = ExitStack()
        squares1 = sb("squares1", [P, T * D], at=l1)
        h2h = sb("h2h", [P, DC, SEQ], f32r, at=l1)
        h2l = sb("h2l", [P, DC, SEQ], f32r, at=l1)
        l1.close()
        ffn = ExitStack()
        fs = sb("fs", [P, 2, 2 * SEQ], at=ffn)
        fg = sb("fg", [P, 2, 2 * SEQ], at=ffn)
        fgh = sb("fgh", [P, 2, 2 * SEQ], f32r, at=ffn)
        fgl = sb("fgl", [P, 2, 2 * SEQ], f32r, at=ffn)
        ffn.close()
        pre.close()
        moe = ctx.enter_context(ExitStack())
        wh_b = sb("wh_b", [P, SPLIT, UNIT], f32r, at=moe)
        wl_b = sb("wl_b", [P, SPLIT, UNIT], f32r, at=moe)
        ms = sb("ms", [P, 2, EW], at=moe)
        mg = sb("mg", [P, EW], at=moe)
        gth = sb("gth", [P, EW], f32r, at=moe)
        gtl = sb("gtl", [P, EW], f32r, at=moe)
        ye = sb("ye", [P, D], at=moe)
        cmb = sb("cmb", [P, SEQ], at=moe)
        pick = sb("pick", [P, T, P], at=moe)
        gpick = sb("gpick", [P, T, P], at=moe)
        cur = sb("cur", [P, 3, T], at=moe)
        ps = [ctx.enter_context(nc.psum_tensor(f"ps{i}", [P, 512], fp32)) for i in range(8)]

        ident = cst[:, C_ID:C_ID + P]
        tri = cst[:, C_TRI:C_TRI + P]
        iota = cst[:, C_IOTA:C_IOTA + P]
        ones = cst[:, C_ONES:C_ONES + P]
        ropc = cst[:, C_ROPC:C_ROPC + T * ROPE].rearrange("p (t r) -> p t r", t=T)
        rops = cst[:, C_ROPS:C_ROPS + T * ROPE].rearrange("p (t r) -> p t r", t=T)
        rev = cst[:, C_REV:C_REV + T * NE].rearrange("p (t e) -> p t e", t=T)
        mask_row = cst[:, C_MA:C_MA + P]
        mask_col = cst[:, C_MB:C_MB + CHUNK]

        q1 = q_all[:, :, 0:D]
        k1 = kv_all[:, :, 0:D]
        v1 = kv_all[:, :, D:2 * D]

        def heads(a, w, lo=0, hi=None):
            return a.rearrange("p t (h w) -> p t h w", w=w)[:, :, :, lo:w if hi is None else hi]

        raw_here = [sem(f"raw_here{i}") for i in range(RAW)]
        hi_done = sem("hi_done")
        lo_done = sem("lo_done")
        unit_used = sem("unit_used")
        x_here = sem("x_here")
        c_here = sem("c_here")
        g_here = sem("g_here")
        hg_here = sem("hg_here")
        wr_here = sem("wr_here")
        gcol_tr = sem("gcol_tr")
        gcol_done = sem("gcol_done")
        pool_init = sem("pool_init")
        rope_tab = sem("rope_tab")
        ss_done = sem("ss_done")
        ss_lat = sem("ss_lat")
        p_step = sem("p_step")
        rstd_done = sem("rstd_done")
        rstd_lat = sem("rstd_lat")
        tn_done = sem("tn_done")
        tr_done = sem("tr_done")
        th_done = sem("th_done")
        tl_done = sem("tl_done")
        xr_done = sem("xr_done")
        lat_tn = sem("lat_tn")
        lat_tr = sem("lat_tr")
        lat_h = sem("lat_h")
        lat_l = sem("lat_l")
        pj_a = [sem("pj_a0"), sem("pj_a1")]
        pj_v = [sem("pj_v0"), sem("pj_v1")]
        sq_done = [sem("sq_done0"), sem("sq_done1")]
        sh_done = [sem("sh_done0"), sem("sh_done1")]
        rs_done = [sem("rs_done0"), sem("rs_done1")]
        rq_done = sem("rq_done")
        rk_done = sem("rk_done")
        A = []
        for la in range(2):
            A.append({k: sem(f"{k}_{la}") for k in (
                "qn", "kn",
                "tq", "tk",
                "qT", "kT",
                "s",
                "sb",
                "nm",
                "ex",
                "pt",
                "pa", "pv",
                "o",
                "ri",
                "oo")})
        wide_done = sem("wide_done")
        bias_here = [sem("bias_here0"), sem("bias_here1")]
        v_step = sem("v_step")
        f_s = sem("f_s")
        f_g = sem("f_g")
        f_gh = sem("f_gh")
        f_gl = sem("f_gl")
        wrh_done = sem("wrh_done")
        wrl_done = sem("wrl_done")
        lg_mm = sem("lg_mm")
        v_done = sem("v_done")
        e_done = sem("e_done")
        sel_done = sem("sel_done")
        pos_mm = sem("pos_mm")
        tab_done = sem("tab_done")
        m_zero = sem("m_zero")
        m_s = sem("m_s")
        m_g = sem("m_g")
        m_t = sem("m_t")
        m_gh = sem("m_gh")
        m_gl = sem("m_gl")
        m_ye = sem("m_ye")
        m_gat = sem("m_gat")
        m_hh = sem("m_hh")
        m_hl = sem("m_hl")
        m_cur = sem("m_cur")
        m_pick = sem("m_pick")
        m_c = sem("m_c")
        m_cs = sem("m_cs")
        m_cmb = sem("m_cmb")
        m_add = sem("m_add")
        out_done = sem("out_done")

        TURN_BANKS = DC // 2
        TURN = {"n0": 0, "a0": 1, "n1": 2, "n2": 3, "a1": 4, "n3": 5}

        def split_slot(n):
            return wh_a[:, n % SPLIT, :], wl_a[:, n % SPLIT, :]

        def moe_slot(k):
            s = k % (2 * SPLIT)
            h, l = (wh_a, wl_a) if s < SPLIT else (wh_b, wl_b)
            return h[:, s % SPLIT, :], l[:, s % SPLIT, :]

        def latent_out(i):
            if i < 6:
                return U_UQ + i // 2 + 1, q_all[:, i % 2, (i // 2) * 512:(i // 2 + 1) * 512]
            k = (i - 6) // 2
            return U_UKV + (i - 6) // 4 + 1, kv_all[:, i % 2, k * 512:(k + 1) * 512]

        block = ctx.enter_context(nc.Block())

        @block.sync
        def _(sp):
            for t in range(T):
                sp.dma_start(xr[:, t, :], x_v[:, t, :]).then_inc(x_here, 16)

            def load(n, src, shape, j=0, j_units=0, slot_n=None):
                a, b = shape
                dst = raw[:, n % RAW, 0:a * b].rearrange("p (a b) -> p a b", a=a)
                if n >= RAW:
                    sp.wait_ge(lo_done, n - RAW + 1 + j * j_units)
                sp.dma_start(dst, src).then_inc(raw_here[n % RAW], 16)

            for h in range(2):
                load(U_DQ + h, dq_v[:, 4 * h:4 * h + 4, :], (4, Q_LORA))
            for h in range(2):
                load(U_DKV + h, dkv_v[:, 4 * h:4 * h + 4, :], (4, KV_LORA + ROPE))
            for n in range(3):
                load(U_UQ + n, uq_v[:, :, n * 512:(n + 1) * 512], (QC, 512))
            for n in range(2):
                load(U_UKV + n, ukv_v[:, :, n * 1024:(n + 1) * 1024], (KVC, 1024))
            for n in range(2):
                for h in range(2):
                    load(U_WO0 + 2 * n + h, oa_v[:, 4 * h:4 * h + 4, n * 512:(n + 1) * 512], (4, 512))
            for w, v in enumerate((w1_v, w3_v)):
                load(U_FFN + w, v[:, :, 0:FW], (DC, FW))
            with sp.Fori(0, (FSTEPS - 1) // 2) as j:
                for u in range(2):
                    n = U_FFN + 2 + 3 * u
                    for w, v in enumerate((w1_v, w3_v)):
                        load(n + w, v[:, :, ds(j * (2 * FW) + (1 + u) * FW, FW)], (DC, FW), j, 6)
                    load(n + 2, w2_v[:, ds(j * 4 + 2 * u, 2), :], (2, D), j, 6)
            load(U_L1 - 1, w2_v[:, 2 * (FSTEPS - 1):2 * FSTEPS, :], (2, D))
            for w in range(4):
                for n in range(2):
                    for h in range(2):
                        load(U_L1 + 4 * w + 2 * n + h, l1_v[w][:, 4 * h:4 * h + 4, n * 512:(n + 1) * 512], (4, 512))

            def expert(e, j):
                k = 0
                for c in range(ESTEPS + 1):
                    if c < ESTEPS:
                        for v in (m1_v, m3_v):
                            for h in range(2):
                                load(U_MOE + k, v[:, ds(e * DC + 4 * h, 4), c * EW:(c + 1) * EW], (4, EW), j, U_RUN)
                                k += 1
                    if c:
                        for n in range(2):
                            load(U_MOE + k, m2_v[:, ds(e * (EFF // P) + 4 * (c - 1), 4), n * 512:(n + 1) * 512],
                                 (4, 512), j, U_RUN)
                            k += 1
                assert k == U_RUN

            with sp.Fori(0, NE) as e:
                expert(e, e)
            sp.wait_ge(tab_done, 1)
            extra = sp.value_load(tab[0:1, 1:2], min_val=0, max_val=V_EXTRA)
            with sp.If(extra > 0):
                with sp.Fori(0, extra) as i:
                    e = sp.value_load(tab[0:1, ds(i + 2, 1)], min_val=0, max_val=NE - 1)
                    expert(e, i + NE)
            runs = sp.value_load(tab[0:1, 0:1], min_val=NE, max_val=NE + V_EXTRA)
            sp.wait_ge(m_add, runs * 4 + 4)
            for t in range(T):
                sp.dma_start(out_v[:, t, :], xr[:, t, :]).then_inc(out_done, 16)
            sp.wait_ge(out_done, 16 * T)

        @block.gpsimd
        def _(pool):
            steps = [0]

            def chain(ins):
                steps[0] += 1
                ins.then_inc(p_step, 1)
                pool.wait_ge(p_step, steps[0])

            nc.gpsimd.memset(negh[:], -0.5).then_inc(pool_init, 1)
            nc.gpsimd.memset(qkg[:, 0, :], 1.0).then_inc(pool_init, 1)
            pool.wait_ge(pool_init, 2)
            with nc.allow_non_contiguous_dma("a few gains"):
                for i, g in enumerate((g_qn, g_kn)):
                    pool.dma_start(qkg[0:NOPE, 0, i:i + 1], g[0:1, 0:NOPE].rearrange("a p -> p a")).then_inc(hg_here, 16)
                for i, g in enumerate((g_qq, g_kk)):
                    for h in range(2):
                        pool.dma_start(qkg[h * HD:(h + 1) * HD, 1, i:i + 1], g.rearrange("a p -> p a")).then_inc(hg_here, 16)
            for i, g in enumerate((g_qn, g_kn)):
                for s, parts in enumerate((((0, NOPE, ROPE),), ((0, NOPE + HALF, HALF), (HALF, NOPE, HALF)))):
                    for at, src, n in parts:
                        pool.dma_start(pe_g[:, i, s, at:at + n],
                                       g[0:1, src:src + n].to_broadcast([P, n])).then_inc(hg_here, 16)
            pool.wait_ge(hg_here, 16 * 12)
            pool.wait_ge(c_here, 16)
            for i in range(2):
                for s, tab_ in enumerate((ropc, rops)):
                    chain(nc.gpsimd.tensor_tensor(ropt[:, i, s, :, :], tab_,
                                                  pe_g[:, i, s:s + 1, :].to_broadcast([P, T, ROPE]), ALU.mult))
            chain(nc.gpsimd.tensor_scalar(ropt[:, 0, :, :, :], ropt[:, 0, :, :, :], QK ** -0.5, None, ALU.mult))
            nc.gpsimd.tensor_scalar(qkg[0:NOPE, 0, 0:1], qkg[0:NOPE, 0, 0:1], QK ** -0.5, None, ALU.mult).then_inc(rope_tab, 1)
            nc.gpsimd.tensor_scalar(qkg[:, 1, 0:1], qkg[:, 1, 0:1], HD ** -0.5, None, ALU.mult).then_inc(rope_tab, 1)

            def root(dst, src, n):
                chain(nc.gpsimd.tensor_scalar(dst, src, 1.0 / n, EPS, ALU.mult, ALU.add))
                return nc.gpsimd.tensor_tensor(dst, dst, negh[:, 0:dst.shape[1]], ALU.pow)

            def norm(m):
                pool.wait_ge(ss_done, 2 * (m + 1))
                root(rstd[:, 0:T], ss[:, 0:T], D).then_inc(rstd_done, 1)

            norm(0)
            pool.wait_ge(ss_lat, 4)
            root(rstd[:, 0:T], ss[:, 0:T], Q_LORA).then_inc(rstd_lat, 1)
            root(rstd[:, T:2 * T], ss[:, T:2 * T], KV_LORA).then_inc(rstd_lat, 1)
            for t in range(T):
                pool.wait_ge(sq_done[0], t + 1)
                qp = heads(q_all[:, t:t + 1, :], QK, NOPE)[:, 0]

                def fac(s, a, b):
                    return ropt[:, 0, s, t:t + 1, a:b].to_broadcast([P, HEADS, b - a])

                nc.gpsimd.tensor_tensor(roptmp[:, 0], qp, fac(0, 0, ROPE), ALU.mult)
                nc.gpsimd.tensor_tensor(roptmp[:, 1, :, 0:HALF], qp[:, :, HALF:ROPE], fac(1, 0, HALF), ALU.mult)
                chain(nc.gpsimd.tensor_tensor(roptmp[:, 1, :, HALF:ROPE], qp[:, :, 0:HALF], fac(1, HALF, ROPE), ALU.mult))
                nc.gpsimd.tensor_tensor(qp, roptmp[:, 0], roptmp[:, 1], ALU.add).then_inc(rq_done, 1)
                pool.wait_ge(rq_done, t + 1)
            pool.wait_ge(sq_done[0], 4)
            kt_ = roptmp[:, 1, 0:T, :]
            nc.gpsimd.tensor_tensor(roptmp[:, 0, 0:T, :], kpe[:], ropt[:, 1, 0], ALU.mult)
            nc.gpsimd.tensor_tensor(kt_[:, :, 0:HALF], kpe[:, :, HALF:ROPE], ropt[:, 1, 1, :, 0:HALF], ALU.mult)
            chain(nc.gpsimd.tensor_tensor(kt_[:, :, HALF:ROPE], kpe[:, :, 0:HALF], ropt[:, 1, 1, :, HALF:ROPE], ALU.mult))
            nc.gpsimd.tensor_tensor(kpr[:], roptmp[:, 0, 0:T, :], kt_, ALU.add).then_inc(rk_done, 1)
            pool.wait_ge(rk_done, 1)

            def head_roots(la, n):
                pool.wait_ge(sh_done[la], 4)
                root(rsh[:].rearrange("p a t h -> p (a t h)"), ssh[:].rearrange("p a t h -> p (a t h)"), n).then_inc(rs_done[la], 1)
                pool.wait_ge(rs_done[la], 1)

            def scale_k(la, p, par, first=False):
                if not first:
                    pool.wait_ge(A[la]["tk"], p - 1)
                if la == 0:
                    dst = kn[:, par].rearrange("p t (h w) -> p t h w", h=2)
                    r = rsh[:, 1, :, ds(p * 2, 2)].unsqueeze(3)
                    src = kv_all[:].rearrange("p t (h w) -> p t h w", h=HEADS)[:, :, ds(p * 2, 2), 0:NOPE]
                    nc.gpsimd.tensor_tensor(dst[:, :, :, 0:NOPE], src, r.to_broadcast([P, T, 2, NOPE]), ALU.mult)
                    nc.gpsimd.tensor_tensor(dst[:, :, :, NOPE:QK], kpr[:].unsqueeze(2).to_broadcast([P, T, 2, ROPE]),
                                            r.to_broadcast([P, T, 2, ROPE]), ALU.mult).then_inc(A[la]["kn"], 1)
                else:
                    dst = kn[:, par, :, 0:2 * HD].rearrange("p t (h w) -> p t h w", h=2)
                    r = rsh[:, 1, :, ds(p * 2, 2)].unsqueeze(3)
                    src = k1.rearrange("p t (h w) -> p t h w", h=HEADS)[:, :, ds(p * 2, 2), :]
                    nc.gpsimd.tensor_tensor(dst, src, r.to_broadcast([P, T, 2, HD]), ALU.mult).then_inc(A[la]["kn"], 1)

            def attention(la):
                scale_k(la, 0, 0, first=True)
                scale_k(la, 1, 1, first=True)
                with pool.Fori(0, PAIRS // 2 - 1) as j:
                    for u in range(2):
                        scale_k(la, j * 2 + (2 + u), u)

            head_roots(0, QK)
            attention(0)
            norm(1)
            norm(2)
            head_roots(1, HD)
            attention(1)
            norm(3)

        @block.scalar
        def _(act):
            act.dma_start(cst[:], consts).then_inc(c_here, 16)
            for at, g, n in ((G_ATT, attn_norm, 2 * DC), (G_FFN, ffn_norm, 2 * DC), (G_CQ, g_cq, QC), (G_CKV, g_ckv, KVC)):
                act.dma_start(grow[at:at + n, :], g.rearrange("l (c p) -> (l c) p", p=P)).then_inc(g_here, 16)
            act.dma_start(grow[G_KV:G_KV + DC, :], kv_norm.rearrange("a (c p) -> (a c) p", p=P)).then_inc(g_here, 16)
            act.dma_start(wr[:], rt_v).then_inc(wr_here, 16)

            def hi(n, j=0, j_units=0, w=None):
                moe_unit = n - U_MOE
                dst = moe_slot(moe_unit)[0] if moe_unit >= 0 else split_slot(n)[0]
                w = width(n) if w is None else w
                act.wait_ge(raw_here[n % RAW], 16 * (n // RAW + 1) + j * (16 * j_units // RAW))
                if moe_unit >= 0:
                    act.wait_ge(unit_used, n - 2 * SPLIT + 1 + j * j_units)
                elif n >= SPLIT:
                    act.wait_ge(unit_used, n - SPLIT + 1 + j * j_units)
                nc.scalar.activation(dst[:, 0:w], raw[:, n % RAW, 0:w], ACT.Copy).then_inc(hi_done, 1)

            def sum_squares(m, first):
                for t in range(T):
                    if first:
                        act.wait_ge(x_here, 16 * T)
                    nc.scalar.activation(tn[:, t, :], xr[:, t, :], ACT.Square, accum_out=ss[:, t:t + 1]).then_inc(ss_done, 1)

            def turn_out(name, dsts):
                k = TURN[name]
                for b in range(TURN_BANKS):
                    act.wait_ge(tr_done, TURN_BANKS * k + b + 1)
                    for cc in range(2):
                        c = 2 * b + cc
                        for dst, g in dsts:
                            kw = {} if g is None else {"scale": gcol[:, g + c:g + c + 1]}
                            last = nc.scalar.activation(dst[:, c, :], ps[b][:, cc * SEQ:(cc + 1) * SEQ], ACT.Copy, **kw)
                    last.then_inc(th_done, 1)

            sum_squares(0, True)
            hi(0)
            hi(1)
            act.wait_ge(gcol_done, 1)
            turn_out("n0", [(hth, G_ATT)])
            hi(2)
            hi(3)
            act.wait_ge(unit_used, U_UQ)
            for t in range(T):
                nc.scalar.activation(squares[:, t * Q_LORA:(t + 1) * Q_LORA], ps[4 + t][:, 0:Q_LORA], ACT.Square,
                                     accum_out=ss[:, t:t + 1]).then_inc(ss_lat, 1)
            for t in range(T):
                nc.scalar.activation(squares[:, T * Q_LORA + t * KV_LORA:T * Q_LORA + (t + 1) * KV_LORA], ps[6 + t][:, 0:KV_LORA], ACT.Square,
                                     accum_out=ss[:, T + t:T + t + 1]).then_inc(ss_lat, 1)
            hi(4)
            hi(5)
            for b in range(3):
                act.wait_ge(lat_tr, b + 1)
                for cc in range(2 if b < 2 else 1):
                    c = 2 * b + cc
                    last = nc.scalar.activation(ch[:, c, :], ps[b][:, cc * SEQ:(cc + 1) * SEQ], ACT.Copy,
                                                scale=gcol[:, G_CQ + c:G_CQ + c + 1])
                last.then_inc(lat_h, 1)
            for i in range(14):
                if i % 2 == 0:
                    act.wait_ge(unit_used, latent_out(i)[0])
                    nc.scalar.activation(latent_out(i)[1], ps[4 + i % 4][:, :], ACT.Copy).then_inc(pj_a[0], 1)
                if i in (1, 3, 5, 9):
                    hi({1: 6, 3: 7, 5: 8, 9: 9}[i])
            hi(10)
            hi(11)
            act.wait_ge(ss_lat, 4)
            act.wait_ge(pj_a[0], 7)
            act.wait_ge(pj_v[0], 7)
            for t in range(T):
                nc.scalar.activation(squares[:, t * HEADS * QK:(t + 1) * HEADS * QK], q_all[:, t, :], ACT.Square).then_inc(sq_done[0], 1)
            for t in range(T):
                act.wait_ge(sh_done[0], t + 1)
                nc.scalar.activation(squares[:, t * HEADS * QK:t * HEADS * QK + HEADS * NOPE].rearrange("p (h w) -> p h w", w=NOPE),
                                     heads(kv_all[:, t:t + 1, :], NOPE + VDIM, 0, NOPE)[:, 0], ACT.Square)
                nc.scalar.activation(squares[:, t * HEADS * QK + HEADS * NOPE:t * HEADS * QK + HEADS * NOPE + ROPE],
                                     kpe[:, t, :], ACT.Square, accum_out=ss[:, t:t + 1]).then_inc(sq_done[0], 1)

            def attention(la):
                a = A[la]
                w = QK if la == 0 else P
                n = 2 * SEQ if la == 0 else SEQ

                def load_bias(p, par, wait=True):
                    if wait:
                        act.wait_ge(a["ex"], p * 2 - 2)
                    act.dma_start(bias[:, par, :, :], bias_wide[ds(p * 2, 2), :, :].rearrange("h q k -> q h k")).then_inc(bias_here[par], 16)

                def q_out(p, par):
                    act.wait_ge(a["tq"], p + 1)
                    nc.scalar.activation(qT[0:w, par, 0:n], ps[0][0:w, 0:n], ACT.Copy,
                                         scale=qkg[0:w, la, 0:1]).then_inc(a["qT"], 1)

                def probs(p, par):
                    for h in range(2):
                        act.wait_ge(a["nm"], p * 2 + (h + 1))
                        src = ps[2 + h] if la == 0 else bias[:, par, h, :]
                        for t, (lo_, n_) in enumerate(((0, P), (P, SEQ))):
                            last = nc.scalar.activation(prob[:, par, h, lo_:lo_ + n_], src[:, lo_:lo_ + n_], ACT.Exp,
                                                        bias=nmax[:, par, t, h:h + 1], accum_out=rsum[:, par, t, h:h + 1])
                        last.then_inc(a["ex"], 1)

                def pt_out(p, par):
                    act.wait_ge(a["pt"], p * 2 + 1)
                    nc.scalar.activation(probT[:, par, 0, :], ps[4][:, 0:SPAN], ACT.Copy).then_inc(a["pa"], 1)

                def step(p, par):
                    q_out(p + 1, 1 - par)
                    pt_out(p, par)
                    probs(p + 1, 1 - par)

                if la == 1:
                    act.wait_ge(wide_done, 32)
                    load_bias(0, 0, wait=False)
                    load_bias(1, 1, wait=False)
                q_out(0, 0)
                probs(0, 0)
                with act.Fori(0, PAIRS // 2 - 1) as j:
                    for u in range(2):
                        step(j * 2 + u, u)
                        if la == 1:
                            load_bias(j * 2 + (u + 2), u, wait=True)
                step(PAIRS - 2, 0)
                pt_out(PAIRS - 1, 1)

            for at, skip, keys in ((0, P, P), (P, 0, SEQ)):
                src = bass.AP(tensor=bias_rows.tensor, offset=P - 1 + skip, ap=[[SPAN, HEADS], [-1, P], [1, keys]])
                act.dma_start(bias_wide[:, :, at:at + keys], src).then_inc(wide_done, 16)
            act.wait_ge(rope_tab, 2)
            attention(0)
            turn_out("a0", [(hth, None)])
            for n in range(U_WO0 + 3, U_FFN + 3):
                hi(n)
            act.wait_ge(xr_done, 4)
            sum_squares(1, False)
            turn_out("n1", [(hth, G_FFN)])

            def f_silu(c, par):
                act.wait_ge(unit_used, U_FFN + 1 if isinstance(c, int) else c * 3 + U_FFN)
                nc.scalar.activation(fs[:, par, :], ps[par][:, :], ACT.Silu).then_inc(f_s, 1)

            def f_hi(c, par):
                act.wait_ge(f_g, c + 1)
                nc.scalar.activation(fgh[:, par, :], fg[:, par, :], ACT.Copy).then_inc(f_gh, 1)

            f_silu(0, 0)
            hi(U_FFN + 3)
            f_hi(0, 0)
            with act.Fori(0, (FSTEPS - 1) // 2) as j:
                for u in range(2):
                    n = U_FFN + 4 + 3 * u
                    hi(n, j, 6)
                    hi(n + 1, j, 6)
                    f_silu(j * 2 + (u + 1), 1 - u)
                    hi(n + 2, j, 6)
                    f_hi(j * 2 + (u + 1), 1 - u)
            hi(U_L1 + 1)
            act.wait_ge(xr_done, 8)
            sum_squares(2, False)
            turn_out("n2", [(hth, G_ATT + DC), (h2h, G_KV)])
            for g in range(6):
                hi(U_L1 + 2 + 2 * g)
                hi(U_L1 + 3 + 2 * g)
                act.wait_ge(unit_used, U_L1 + 2 + 2 * g)
                nc.scalar.activation((q1, k1, v1)[g // 2][:, 0, (g % 2) * 512:(g % 2 + 1) * 512], ps[4 + g % 2 * 2][:, :],
                                     ACT.Copy).then_inc(pj_a[1], 1)
                if g in (1, 3):
                    act.wait_ge(pj_a[1], g + 1)
                    act.wait_ge(pj_v[1], g + 1)
                    if g == 3:
                        act.wait_ge(sh_done[1], 2)
                    for t in range(T):
                        nc.scalar.activation(squares1[:, t * D:(t + 1) * D], (q1, k1)[g // 2][:, t, :],
                                             ACT.Square).then_inc(sq_done[1], 1)
            hi(U_MOE - 2)
            attention(1)
            turn_out("a1", [(hth, None)])
            hi(U_MOE - 1)
            act.wait_ge(wr_here, 16)
            nc.scalar.activation(wrh[:], wr[:], ACT.Copy).then_inc(wrh_done, 1)
            act.wait_ge(xr_done, 12)
            sum_squares(3, False)
            turn_out("n3", [(hth, G_FFN + DC)])
            act.wait_ge(v_done, 1)
            nc.scalar.activation(tops[:, 2, :], tops[:, 3, :], ACT.Exp).then_inc(e_done, 1)

            act.wait_ge(tab_done, 1)
            runs = act.value_load(tab[0:1, 0:1], min_val=NE, max_val=NE + V_EXTRA)

            def gathered(v):
                for g in range(2):
                    act.wait_ge(m_gat, v * 2 + (g + 1))
                    for cc in range(4):
                        c = 4 * g + cc
                        last = nc.scalar.activation(hth[:, c, 0:P], ps[7 - g][:, cc * P:(cc + 1) * P], ACT.Copy,
                                                    scale=gcol[:, G_FFN + DC + c:G_FFN + DC + c + 1])
                    last.then_inc(m_hh, 1)

            def y_out(v):
                act.wait_ge(unit_used, v * U_RUN + U_MOE)
                for n in range(2):
                    last = nc.scalar.activation(ye[:, n * 512:(n + 1) * 512], ps[4 + n][:, :], ACT.Copy)
                last.then_inc(m_ye, 1)

            def gt_hi(v, c):
                act.wait_ge(m_t, v * ESTEPS + (c + 1))
                nc.scalar.activation(gth[:], ps[6 + c % 2][:, :], ACT.Copy).then_inc(m_gh, 1)

            gathered(0)
            act.wait_ge(unit_used, U_MOE)
            act.wait_ge(m_zero, 1)
            with act.Fori(0, runs) as v:
                def mhi(k):
                    if k < U_RUN:
                        hi(U_MOE + k, v, U_RUN, UNIT)

                for k in range(4):
                    mhi(k)
                    if k == 1:
                        y_out(v)
                k = 0
                for c in range(ESTEPS):
                    mhi(k + 4)
                    mhi(k + 5)
                    if c:
                        gt_hi(v, c - 1)
                    act.wait_ge(unit_used, v * U_RUN + (U_MOE + k + 2))
                    nc.scalar.activation(ms[:, c % 2, :], ps[c % 2][:, :], ACT.Silu).then_inc(m_s, 1)
                    for i in range(2, 4 if c == 0 else 6):
                        mhi(k + 4 + i)
                    k += 4 if c == 0 else 6
                gt_hi(v, ESTEPS - 1)
                act.wait_ge(m_c, v + 1)
                nc.scalar.activation(cmb[:], ps[1][:, 0:SEQ], ACT.Copy).then_inc(m_cs, 1)
                gathered(v + 1)
            y_out(runs)

        @block.vector
        def _(dve):
            steps = [0]

            def chain(ins):
                steps[0] += 1
                ins.then_inc(v_step, 1)
                dve.wait_ge(v_step, steps[0])


            def lo(n, j=0, j_units=0, w=None):
                moe_unit = n - U_MOE
                h, l = moe_slot(moe_unit) if moe_unit >= 0 else split_slot(n)
                w = width(n) if w is None else w
                dve.wait_ge(hi_done, n + 1 + j * j_units)
                nc.vector.tensor_tensor(l[:, 0:w], raw[:, n % RAW, 0:w], h[:, 0:w].bitcast(fp32),
                                        ALU.subtract).then_inc(lo_done, 1)

            def normalise(m):
                dve.wait_ge(rstd_done, m + 1)
                for t in range(T):
                    nc.vector.tensor_scalar(tn[:, t, :], xr[:, t, :], rstd[:, t:t + 1], None, ALU.mult).then_inc(tn_done, 1)

            def turn_out(name, dsts):
                k = TURN[name]
                for b in range(TURN_BANKS):
                    dve.wait_ge(th_done, TURN_BANKS * k + b + 1)
                    for cc in range(2):
                        c = 2 * b + cc
                        src = ps[b][:, cc * SEQ:(cc + 1) * SEQ]
                        for h, l, g in dsts:
                            if g is None:
                                last = nc.vector.tensor_tensor(l[:, c, :], src, h[:, c, :].bitcast(fp32), ALU.subtract)
                            else:
                                last = nc.vector.scalar_tensor_tensor(l[:, c, :], src, gcol[:, g + c:g + c + 1],
                                                                      h[:, c, :].bitcast(fp32), ALU.mult, ALU.subtract)
                    last.then_inc(tl_done, 1)

            def add_residual(used):
                for n in range(2):
                    dve.wait_ge(unit_used, used[n])
                    for t in range(T):
                        i = 2 * n + t
                        piece = xr[:, t, n * 512:(n + 1) * 512]
                        nc.vector.tensor_tensor(piece, ps[4 + i][:, :], piece, ALU.add).then_inc(xr_done, 1)

            dve.wait_ge(gcol_tr, 1)
            nc.vector.tensor_copy(gcol[:], ps[7][:, 0:G_ALL]).then_inc(gcol_done, 1)
            normalise(0)
            lo(0)
            lo(1)
            dve.wait_ge(gcol_done, 1)
            turn_out("n0", [(hth, htl, G_ATT)])
            lo(2)
            lo(3)
            cq = tn[:, :, 0:Q_LORA]
            ckv = tn[:, :, Q_LORA:Q_LORA + KV_LORA]
            dve.wait_ge(rstd_lat, 2)
            for t in range(T):
                nc.vector.tensor_scalar(cq[:, t, :], ps[4 + t][:, 0:Q_LORA], rstd[:, t:t + 1], None, ALU.mult).then_inc(lat_tn, 1)
            for t in range(T):
                nc.vector.tensor_copy(kpe[:, t, :], ps[6 + t][:, KV_LORA:KV_LORA + ROPE])
                nc.vector.tensor_scalar(ckv[:, t, :], ps[6 + t][:, 0:KV_LORA], rstd[:, T + t:T + t + 1], None, ALU.mult).then_inc(lat_tn, 1)
            lo(4)
            lo(5)
            for b in range(3):
                dve.wait_ge(lat_h, b + 1)
                for cc in range(2 if b < 2 else 1):
                    c = 2 * b + cc
                    last = nc.vector.scalar_tensor_tensor(cl[:, c, :], ps[b][:, cc * SEQ:(cc + 1) * SEQ],
                                                          gcol[:, G_CQ + c:G_CQ + c + 1], ch[:, c, :].bitcast(fp32),
                                                          ALU.mult, ALU.subtract)
                last.then_inc(lat_l, 1)
            for i in range(14):
                if i % 2 == 1:
                    dve.wait_ge(unit_used, latent_out(i)[0])
                    nc.vector.tensor_copy(latent_out(i)[1], ps[4 + i % 4][:, :]).then_inc(pj_v[0], 1)
                if i in (1, 3, 5, 9):
                    lo({1: 6, 3: 7, 5: 8, 9: 9}[i])
            lo(10)
            lo(11)
            for t in range(T):
                dve.wait_ge(sq_done[0], t + 1)
                nc.vector.reduce_sum(ssh[:, 0, t, :], squares[:, t * HEADS * QK:(t + 1) * HEADS * QK].rearrange("p (h w) -> p h w", w=QK),
                                     AX).then_inc(sh_done[0], 1)
            for t in range(T):
                dve.wait_ge(sq_done[0], T + t + 1)
                chain(nc.vector.reduce_sum(ssh[:, 1, t, :],
                                           squares[:, t * HEADS * QK:t * HEADS * QK + HEADS * NOPE].rearrange("p (h w) -> p h w", w=NOPE), AX))
                nc.vector.tensor_scalar(ssh[:, 1, t, :], ssh[:, 1, t, :], ss[:, t:t + 1], None, ALU.add).then_inc(sh_done[0], 1)

            def attention(la):
                a = A[la]
                w = QK if la == 0 else P
                n = 2 * SEQ if la == 0 else SEQ
                hw = QK if la == 0 else HD

                def scale_q(p, par, first=False):
                    if not first:
                        dve.wait_ge(a["tq"], p - 1)
                    dst = qn[:, par, :, 0:2 * hw].rearrange("p t (h w) -> p t h w", h=2)
                    src = (q_all[:] if la == 0 else q1).rearrange("p t (h w) -> p t h w", h=HEADS)[:, :, ds(p * 2, 2), :]
                    nc.vector.tensor_tensor(dst, src, rsh[:, 0, :, ds(p * 2, 2)].unsqueeze(3).to_broadcast([P, T, 2, hw]),
                                            ALU.mult).then_inc(a["qn"], 1)

                def k_out(p, par):
                    dve.wait_ge(a["tk"], p + 1)
                    nc.vector.tensor_scalar(kT[0:w, par, 0:n], ps[1][0:w, 0:n], qkg[0:w, la, 1:2], None,
                                            ALU.mult).then_inc(a["kT"], 1)

                def maxima(p, par):
                    for h in range(2):
                        dve.wait_ge(a["s"], p * 2 + (h + 1))
                        src = ps[2 + h]
                        if la == 1:
                            if h == 0:
                                dve.wait_ge(bias_here[par], (p - par) * 8 + 16)
                            src = bias[:, par, h, :]
                            nc.vector.tensor_tensor(src, ps[2 + h][:, 0:SPAN], src, ALU.add).then_inc(a["sb"], 1)
                            dve.wait_ge(a["sb"], p * 2 + (h + 1))
                        for t, (lo_, n_) in enumerate(((0, P), (P, SEQ))):
                            last = nc.vector.tensor_reduce(nmax[:, par, t, h:h + 1], src[:, lo_:lo_ + n_], axis=AX,
                                                           op=ALU.max, negate=True)
                        last.then_inc(a["nm"], 1)

                def pt_out(p, par):
                    dve.wait_ge(a["pt"], p * 2 + 2)
                    nc.vector.tensor_copy(probT[:, par, 1, :], ps[5][:, 0:SPAN]).then_inc(a["pv"], 1)

                def out_(p, par):
                    dve.wait_ge(a["ex"], p * 2 + 2)
                    nc.vector.reciprocal(rinv[:, par], rsum[:, par]).then_inc(a["ri"], 1)
                    dve.wait_ge(a["ri"], p + 1)
                    dve.wait_ge(a["o"], p + 1)
                    nc.vector.tensor_tensor(tn[:].rearrange("p t (h w) -> p t h w", h=HEADS)[:, :, ds(p * 2, 2), :],
                                            ps[6 + par][:, 0:T * 2 * VDIM].rearrange("p (t h w) -> p t h w", t=T, h=2),
                                            rinv[:, par].unsqueeze(3).to_broadcast([P, T, 2, VDIM]),
                                            ALU.mult).then_inc(a["oo"], 1)

                def step(p, par, more=True):
                    if more:
                        scale_q(p + 2, par)
                    k_out(p + 1, 1 - par)
                    pt_out(p, par)
                    maxima(p + 1, 1 - par)
                    out_(p, par)

                scale_q(0, 0, first=True)
                scale_q(1, 1, first=True)
                k_out(0, 0)
                maxima(0, 0)
                with dve.Fori(0, PAIRS // 2 - 1) as j:
                    for u in range(2):
                        step(j * 2 + u, u)
                step(PAIRS - 2, 0, more=False)
                pt_out(PAIRS - 1, 1)
                out_(PAIRS - 1, 1)

            dve.wait_ge(rs_done[0], 1)
            dve.wait_ge(rq_done, 2)
            dve.wait_ge(rope_tab, 2)
            attention(0)
            turn_out("a0", [(hth, htl, None)])
            lo(U_WO0 + 3)
            add_residual((U_WO0 + 2, U_WO0 + 4))
            for n in range(U_FFN, U_FFN + 3):
                lo(n)
            normalise(1)
            turn_out("n1", [(hth, htl, G_FFN)])

            def f_gate(c, par):
                dve.wait_ge(unit_used, U_FFN + 2 if isinstance(c, int) else c * 3 + (U_FFN + 1))
                dve.wait_ge(f_s, c + 1)
                nc.vector.tensor_tensor(fg[:, par, :], ps[2 + par][:, :], fs[:, par, :], ALU.mult).then_inc(f_g, 1)

            def f_lo(c, par):
                dve.wait_ge(f_gh, c + 1)
                nc.vector.tensor_tensor(fgl[:, par, :], fg[:, par, :], fgh[:, par, :].bitcast(fp32), ALU.subtract).then_inc(f_gl, 1)

            f_gate(0, 0)
            lo(U_FFN + 3)
            f_lo(0, 0)
            with dve.Fori(0, (FSTEPS - 1) // 2) as j:
                for u in range(2):
                    n = U_FFN + 4 + 3 * u
                    lo(n, j, 6)
                    lo(n + 1, j, 6)
                    f_gate(j * 2 + (u + 1), 1 - u)
                    lo(n + 2, j, 6)
                    f_lo(j * 2 + (u + 1), 1 - u)
            lo(U_L1 + 1)
            add_residual((U_L1, U_L1))
            normalise(2)
            turn_out("n2", [(hth, htl, G_ATT + DC), (h2h, h2l, G_KV)])
            for g in range(6):
                lo(U_L1 + 2 + 2 * g)
                lo(U_L1 + 3 + 2 * g)
                dve.wait_ge(unit_used, U_L1 + 2 + 2 * g)
                nc.vector.tensor_copy((q1, k1, v1)[g // 2][:, 1, (g % 2) * 512:(g % 2 + 1) * 512],
                                      ps[5 + g % 2 * 2][:, :]).then_inc(pj_v[1], 1)
                if g in (1, 3):
                    for t in range(T):
                        dve.wait_ge(sq_done[1], g - 1 + t + 1)
                        nc.vector.reduce_sum(ssh[:, g // 2, t, :], squares1[:, t * D:(t + 1) * D].rearrange("p (h w) -> p h w", w=HD),
                                             AX).then_inc(sh_done[1], 1)
            lo(U_MOE - 2)
            dve.wait_ge(rs_done[1], 1)
            attention(1)
            turn_out("a1", [(hth, htl, None)])
            lo(U_MOE - 1)
            dve.wait_ge(wrh_done, 1)
            nc.vector.tensor_tensor(wrl[:], wr[:], wrh[:].bitcast(fp32), ALU.subtract).then_inc(wrl_done, 1)
            add_residual((U_MOE - 2, U_MOE))
            normalise(3)
            turn_out("n3", [(hth, htl, G_FFN + DC)])

            def bc(a):
                return a.unsqueeze(2).to_broadcast([P, T, NE])

            V = nc.vector
            sel1, sel2, sel, gate, tmp, posm = (work[:, i] for i in range(6))
            v1_, v2_, e2, dv, g1_, g2_ = (tops[:, i] for i in range(6))
            dve.wait_ge(lg_mm, 1)
            chain(V.tensor_copy(lg[:], ps[4][:, 0:T * NE].rearrange("p (t e) -> p t e", t=T)))

            def first_max(src, val, one_hot):
                chain(V.tensor_reduce(val, src, axis=AX, op=ALU.max))
                chain(V.tensor_tensor(tmp, src, bc(val), ALU.is_equal))
                chain(V.tensor_tensor(tmp, tmp, rev, ALU.mult))
                chain(V.tensor_reduce(g1_, tmp, axis=AX, op=ALU.max))
                chain(V.tensor_tensor(one_hot, tmp, bc(g1_), ALU.is_equal))

            first_max(lg[:], v1_, sel1)
            chain(V.scalar_tensor_tensor(sel2, sel1, -3e38, lg[:], ALU.mult, ALU.add))
            chain(V.tensor_copy(posm, sel2))
            first_max(posm, v2_, sel2)
            V.tensor_tensor(dv, v2_, v1_, ALU.subtract).then_inc(v_done, 1)
            V.tensor_tensor(sel, sel1, sel2, ALU.add).then_inc(sel_done, 1)
            dve.wait_ge(e_done, 1)
            chain(V.tensor_scalar(g1_, e2, 1.0, None, ALU.add))
            chain(V.reciprocal(g1_, g1_))
            chain(V.tensor_tensor(g2_, e2, g1_, ALU.mult))
            chain(V.tensor_tensor(gate, sel1, bc(g1_), ALU.mult))
            chain(V.tensor_tensor(tmp, sel2, bc(g2_), ALU.mult))
            chain(V.tensor_tensor(gate, gate, tmp, ALU.add))
            dve.wait_ge(pos_mm, 1)
            pp = ps[5][:, 0:T * NE].rearrange("p (t e) -> p t e", t=T)
            cnt = ps[5][:, T * NE:(T + 1) * NE]
            chain(V.scalar_tensor_tensor(posm, pp, 1.0, sel, ALU.add, ALU.mult))
            chain(V.tensor_scalar(posm, posm, -1.0, None, ALU.add))
            chain(V.memset(pos_v[:, NE:, :], -1.0))
            chain(V.memset(gate_v[:, NE:, :], 0.0))
            chain(V.tensor_copy(pos_v[:, 0:NE, :].rearrange("p e t -> p t e"), posm))
            chain(V.tensor_copy(gate_v[:, 0:NE, :].rearrange("p e t -> p t e"), gate))
            big, score, hot, m_ = over[:, 0], over[:, 1], over[:, 2], tabf
            chain(V.tensor_scalar(big, cnt, float(P), None, ALU.is_gt))
            chain(V.tensor_tensor(score, big, rev[:, 0, :], ALU.mult))
            chain(V.reduce_sum(tabf[:, 1:2], big, AX))
            chain(V.tensor_scalar(tabf[:, 0:1], tabf[:, 1:2], float(NE), None, ALU.add))
            chain(V.tensor_scalar(sel1, posm, -float(P), None, ALU.add))
            for i in range(V_EXTRA):
                chain(V.tensor_reduce(tabf[:, 5:6], score, axis=AX, op=ALU.max))
                chain(V.tensor_scalar(hot, score, tabf[:, 5:6], None, ALU.is_equal))
                chain(V.tensor_tensor(hot, hot, big, ALU.mult))
                chain(V.tensor_scalar(tabf[:, 2 + i:3 + i], tabf[:, 5:6], -1.0, float(NE), ALU.mult, ALU.add))
                chain(V.tensor_scalar(tabf[:, 2 + i:3 + i], tabf[:, 2 + i:3 + i], float(NE - 1), None, ALU.min))
                hb = over[:, 2:3, :].to_broadcast([P, T, NE])
                chain(V.tensor_tensor(tmp, sel1, hb, ALU.mult))
                chain(V.tensor_reduce(pos_v[:, NE + i, :], tmp, axis=AX, op=ALU.add))
                chain(V.tensor_tensor(tmp, gate, hb, ALU.mult))
                chain(V.tensor_reduce(gate_v[:, NE + i, :], tmp, axis=AX, op=ALU.add))
                chain(V.tensor_tensor(hot, hot, score, ALU.mult))
                chain(V.tensor_tensor(score, score, hot, ALU.subtract))
            V.memset(cmb[:], 0.0).then_inc(m_cs, 1)
            V.tensor_copy(tab[:, 0:5], tabf[:, 0:5]).then_inc(tab_done, 1)
            dve.wait_ge(tab_done, 1)
            runs = dve.value_load(tab[0:1, 0:1], min_val=NE, max_val=NE + V_EXTRA)

            def gathered(v):
                for g in range(2):
                    dve.wait_ge(m_hh, v * 2 + (g + 1))
                    for cc in range(4):
                        c = 4 * g + cc
                        last = V.scalar_tensor_tensor(htl[:, c, 0:P], ps[7 - g][:, cc * P:(cc + 1) * P],
                                                      gcol[:, G_FFN + DC + c:G_FFN + DC + c + 1],
                                                      hth[:, c, 0:P].bitcast(fp32), ALU.mult, ALU.subtract)
                    last.then_inc(m_hl, 1)

            def gt_lo(v, c):
                dve.wait_ge(m_gh, v * ESTEPS + (c + 1))
                V.tensor_tensor(gtl[:], ps[6 + c % 2][:, :], gth[:].bitcast(fp32), ALU.subtract).then_inc(m_gl, 1)

            def add_run(v):
                for n in range(2):
                    for t in range(T):
                        i = 2 * n + t
                        dve.wait_ge(m_cmb, v * 4 + (i + 1))
                        piece = xr[:, t, n * 512:(n + 1) * 512]
                        V.tensor_tensor(piece, ps[6 + i % 2][:, :], piece, ALU.add).then_inc(m_add, 1)

            V.tensor_copy(cur[:, 0, :], pos_v[:, 0, :]).then_inc(m_cur, 1)
            dve.wait_ge(m_cur, 1)
            for t in range(T):
                V.tensor_scalar(pick[:, t, :], iota, cur[:, 0, t:t + 1], None, ALU.is_equal).then_inc(m_pick, 1)

            def one_hots(v):
                dve.wait_ge(m_gat, v * 2 + 2)
                dve.wait_ge(m_pick, v * 4 + 2)
                V.tensor_copy(cur[:, 0:1, :], pos_v[:, ds(v + 1, 1), :]).then_inc(m_cur, 1)
                V.tensor_copy(cur[:, 1:2, :], pos_v[:, ds(v, 1), :]).then_inc(m_cur, 1)
                V.tensor_copy(cur[:, 2:3, :], gate_v[:, ds(v, 1), :]).then_inc(m_cur, 1)
                dve.wait_ge(m_cur, v * 3 + 4)
                for t in range(T):
                    V.tensor_scalar(gpick[:, t, :], iota, cur[:, 1, t:t + 1], cur[:, 2, t:t + 1],
                                    ALU.is_equal, ALU.mult).then_inc(m_pick, 1)
                for t in range(T):
                    V.tensor_scalar(pick[:, t, :], iota, cur[:, 0, t:t + 1], None, ALU.is_equal).then_inc(m_pick, 1)

            gathered(0)
            with dve.Fori(0, runs) as v:
                def mlo(k):
                    if k < U_RUN:
                        lo(U_MOE + k, v, U_RUN, UNIT)

                for k in range(4):
                    mlo(k)
                k = 0
                for c in range(ESTEPS):
                    mlo(k + 4)
                    mlo(k + 5)
                    if c:
                        gt_lo(v, c - 1)
                    else:
                        add_run(v)
                    for i in range(2, 4):
                        mlo(k + 4 + i)
                    if c == 1:
                        one_hots(v)
                    dve.wait_ge(unit_used, v * U_RUN + (U_MOE + k + 4))
                    dve.wait_ge(m_s, v * ESTEPS + (c + 1))
                    V.tensor_tensor(mg[:], ps[2 + c % 2][:, :], ms[:, c % 2, :], ALU.mult).then_inc(m_g, 1)
                    for i in range(4, 4 if c == 0 else 6):
                        mlo(k + 4 + i)
                    k += 4 if c == 0 else 6
                gt_lo(v, ESTEPS - 1)
                gathered(v + 1)
            add_run(runs)

        @block.tensor
        def _(pe):
            mm = nc.tensor.matmul

            def tr(dst, src, np_=P):
                return nc.tensor.transpose(dst, src, ident[0:np_, 0:np_])

            def mm3(dst, xh, xl, wh, wl, start, stop, flip=False):
                for i, (a, b) in enumerate(((xh, wh), (xl, wh), (xh, wl)) if flip else ((xh, wh), (xh, wl), (xl, wh))):
                    last = mm(dst, b if flip else a, a if flip else b, start=start and i == 0, stop=stop and i == 2)
                return last

            def turn(name, waits):
                for s, value in waits:
                    pe.wait_ge(s, value)
                for b in range(TURN_BANKS):
                    for cc in range(2):
                        for t in range(T):
                            c = 2 * b + cc
                            last = tr(ps[b][:, cc * SEQ + t * P:cc * SEQ + (t + 1) * P], tn[:, t, c * P:(c + 1) * P])
                    last.then_inc(tr_done, 1)

            def turned(name):
                pe.wait_ge(tl_done, TURN_BANKS * (TURN[name] + 1))

            def ready(n, j=0, j_units=0):
                pe.wait_ge(lo_done, n + 1 + j * j_units)

            pe.wait_ge(c_here, 16)
            pe.wait_ge(g_here, 16 * 5)
            tr(ps[7][:, 0:G_ALL], grow[:], G_ALL).then_inc(gcol_tr, 1)
            turn("n0", [(tn_done, 2)])
            turned("n0")

            for u, bank, w in ((U_DQ, 4, Q_LORA), (U_DKV, 6, KV_LORA + ROPE)):
                for h in range(2):
                    ready(u + h)
                    wh, wl = split_slot(u + h)
                    for t in range(T):
                        for cc in range(4):
                            c = 4 * h + cc
                            last = mm3(ps[bank + t][:, 0:w], hth[:, c, t * P:(t + 1) * P], htl[:, c, t * P:(t + 1) * P],
                                       wh[:, cc * w:(cc + 1) * w], wl[:, cc * w:(cc + 1) * w], c == 0, c == DC - 1)
                    last.then_inc(unit_used, 1)
            pe.wait_ge(lat_tn, 4)
            for b in range(3):
                for cc in range(2 if b < 2 else 1):
                    c = 2 * b + cc
                    for t in range(T):
                        last = tr(ps[b][:, cc * SEQ + t * P:cc * SEQ + (t + 1) * P], tn[:, t, c * P:(c + 1) * P])
                last.then_inc(lat_tr, 1)
            pe.wait_ge(lat_l, 3)

            def free_bank(i, la):
                if i >= 4:
                    pe.wait_ge((pj_a if i % 2 == 0 else pj_v)[la], (i - 4) // 2 + 1)

            i = 0
            for n in range(3):
                ready(U_UQ + n)
                wh, wl = split_slot(U_UQ + n)
                for t in range(T):
                    free_bank(i, 0)
                    for c in range(QC):
                        last = mm3(ps[4 + i % 4][:, :], ch[:, c, t * P:(t + 1) * P], cl[:, c, t * P:(t + 1) * P],
                                   wh[:, c * 512:(c + 1) * 512], wl[:, c * 512:(c + 1) * 512], c == 0, c == QC - 1)
                    i += 1
                last.then_inc(unit_used, 1)
            for n in range(2):
                ready(U_UKV + n)
                wh, wl = split_slot(U_UKV + n)
                for s in range(2):
                    for t in range(T):
                        free_bank(i, 0)
                        for c in range(KVC):
                            at = c * 1024 + s * 512
                            last = mm3(ps[4 + i % 4][:, :], ch[:, QC + c, t * P:(t + 1) * P], cl[:, QC + c, t * P:(t + 1) * P],
                                       wh[:, at:at + 512], wl[:, at:at + 512], c == 0, c == KVC - 1)
                        i += 1
                last.then_inc(unit_used, 1)

            def attention(la):
                a = A[la]
                hw = QK if la == 0 else HD
                v_src = kv_all[:].rearrange("p t (h w) -> p t h w", h=HEADS) if la == 0 else v1.rearrange("p t (h w) -> p t h w", h=HEADS)
                v_at = NOPE if la == 0 else 0

                def turn_pair(p, par, first=False):
                    for src, bank, made, out_, done in ((qn, 0, "qn", "qT", "tq"), (kn, 1, "kn", "kT", "tk")):
                        pe.wait_ge(a[made], p + 1)
                        if not first:
                            pe.wait_ge(a[out_], p)
                        if la == 0:
                            for h in range(2):
                                for t in range(T):
                                    last = tr(ps[bank][0:QK, h * SEQ + t * P:h * SEQ + (t + 1) * P],
                                              src[:, par, t, h * QK:(h + 1) * QK])
                        else:
                            for t in range(T):
                                last = tr(ps[bank][:, t * P:(t + 1) * P], src[:, par, t, 0:2 * HD])
                        last.then_inc(a[done], 1)

                def scores(p, par, first=False):
                    pe.wait_ge(a["qT"], p + 1)
                    pe.wait_ge(a["kT"], p + 1)
                    for h in range(2):
                        if not first:
                            pe.wait_ge(a["ex" if la == 0 else "sb"], p * 2 + (h - 1))
                        part = slice(0, QK) if la == 0 else slice(h * HD, (h + 1) * HD)
                        off = h * SEQ if la == 0 else 0
                        for t, (lo_, keys) in enumerate(((0, P), (P, SEQ))):
                            mm(ps[2 + h][:, lo_:lo_ + keys], qT[part, par, off + t * P:off + (t + 1) * P],
                               kT[part, par, off:off + keys], start=True, stop=False)
                            last = mm(ps[2 + h][:, lo_ + keys - CHUNK:lo_ + keys], mask_row, mask_col, start=False, stop=True)
                        last.then_inc(a["s"], 1)

                def turn_probs(p, par, first=False):
                    for h in range(2):
                        pe.wait_ge(a["ex"], p * 2 + (h + 1))
                        if not first:
                            pe.wait_ge(a["pa" if h == 0 else "pv"], p)
                        for b in range(3):
                            last = tr(ps[4 + h][:, b * P:(b + 1) * P], prob[:, par, h, b * P:(b + 1) * P])
                        last.then_inc(a["pt"], 1)

                def values(p, par, first=False):
                    pe.wait_ge(a["pa"], p + 1)
                    pe.wait_ge(a["pv"], p + 1)
                    if not first:
                        pe.wait_ge(a["oo"], p - 1)
                    for t in range(T):
                        for h in range(2):
                            dst = ps[6 + par][:, (2 * t + h) * VDIM:(2 * t + h + 1) * VDIM]
                            for kt in range(t + 1):
                                last = mm(dst, probT[:, par, h, (t + kt) * P:(t + kt + 1) * P],
                                          v_src[:, kt:kt + 1, ds(p * 2 + h, 1), v_at:v_at + VDIM],
                                          start=kt == 0, stop=kt == t)
                    last.then_inc(a["o"], 1)

                turn_pair(0, 0, first=True)
                scores(0, 0, first=True)

                def step(p, par, first=False, second=False):
                    turn_pair(p + 1, 1 - par)
                    turn_probs(p, par, first=first)
                    scores(p + 1, 1 - par)
                    values(p, par, first=first or second)

                step(0, 0, first=True)
                step(1, 1, second=True)
                with pe.Fori(1, PAIRS // 2 - 1) as j:
                    for u in range(2):
                        step(j * 2 + u, u)
                step(PAIRS - 2, 0)
                turn_probs(PAIRS - 1, 1)
                values(PAIRS - 1, 1)

            def out_proj(la, u0):
                for n in range(2):
                    for h in range(2):
                        ready(u0 + 2 * n + h)
                        wh, wl = split_slot(u0 + 2 * n + h)
                        for t in range(T):
                            for cc in range(4):
                                c = 4 * h + cc
                                last = mm3(ps[4 + 2 * n + t][:, :], hth[:, c, t * P:(t + 1) * P], htl[:, c, t * P:(t + 1) * P],
                                           wh[:, cc * 512:(cc + 1) * 512], wl[:, cc * 512:(cc + 1) * 512], c == 0, c == DC - 1)
                        last.then_inc(unit_used, 1)

            attention(0)
            turn("a0", [(A[0]["oo"], PAIRS)])
            turned("a0")
            out_proj(0, U_WO0)

            turn("n1", [(tn_done, 4)])
            turned("n1")

            def up(c, par, n, j=0, j_units=0, free=True):
                for w, bank in enumerate((0, 2)):
                    ready(n + w, j, j_units)
                    wh, wl = split_slot(n + w)
                    for f in range(2):
                        for cc in range(DC):
                            at = cc * FW + f * P
                            last = mm3(ps[bank + par][:, f * SEQ:(f + 1) * SEQ], hth[:, cc, :], htl[:, cc, :],
                                       wh[:, at:at + P], wl[:, at:at + P], cc == 0, cc == DC - 1, flip=True)
                    last.then_inc(unit_used, 1)

            def down(c, par, n, first, last_, j=0, j_units=0):
                ready(n, j, j_units)
                pe.wait_ge(f_gl, c + 1)
                wh, wl = split_slot(n)
                for half in range(2):
                    for t in range(T):
                        for f in range(2):
                            g = slice(f * SEQ + t * P, f * SEQ + (t + 1) * P)
                            at = f * D + half * 512
                            last = mm3(ps[4 + 2 * half + t][:, :], fgh[:, par, g], fgl[:, par, g],
                                       wh[:, at:at + 512], wl[:, at:at + 512], first and f == 0, last_ and f == 1)
                last.then_inc(unit_used, 1)

            def ffn_step(c, par, n, first=False, j=0, j_units=0):
                up(c + 1, 1 - par, n, j, j_units)
                down(c, par, n + 2, first, False, j, j_units)

            up(0, 0, U_FFN)
            ffn_step(0, 0, U_FFN + 2, first=True)
            ffn_step(1, 1, U_FFN + 5)
            with pe.Fori(1, (FSTEPS - 1) // 2) as j:
                for u in range(2):
                    ffn_step(j * 2 + u, u, U_FFN + 2 + 3 * u, j=j, j_units=6)
            down(FSTEPS - 1, 0, U_L1 - 1, False, True)

            turn("n2", [(tn_done, 6)])
            turned("n2")
            i = 0
            for w in range(3):
                xh, xl = (hth, htl) if w == 0 else (h2h, h2l)
                for n in range(2):
                    for h in range(2):
                        u = U_L1 + 4 * w + 2 * n + h
                        ready(u)
                        wh, wl = split_slot(u)
                        for t in range(T):
                            if h == 0:
                                free_bank(i + t, 1)
                            for cc in range(4):
                                c = 4 * h + cc
                                last = mm3(ps[4 + (i + t) % 4][:, :], xh[:, c, t * P:(t + 1) * P], xl[:, c, t * P:(t + 1) * P],
                                           wh[:, cc * 512:(cc + 1) * 512], wl[:, cc * 512:(cc + 1) * 512], c == 0, c == DC - 1)
                        last.then_inc(unit_used, 1)
                    i += 2
            attention(1)
            turn("a1", [(A[1]["oo"], PAIRS)])
            turned("a1")
            out_proj(1, U_MOE - 4)

            turn("n3", [(tn_done, 8)])
            turned("n3")
            pe.wait_ge(wrl_done, 1)
            for t in range(T):
                for c in range(DC):
                    last = mm3(ps[4][:, t * NE:(t + 1) * NE], hth[:, c, t * P:(t + 1) * P], htl[:, c, t * P:(t + 1) * P],
                               wrh[:, c, :], wrl[:, c, :], c == 0, c == DC - 1)
            last.then_inc(lg_mm, 1)
            pe.wait_ge(sel_done, 1)
            sel = work[:, 2]
            mm(ps[5][:, 0:NE], tri, sel[:, 0, :], start=True, stop=True)
            for dst, m in ((1, tri), (2, ones)):
                mm(ps[5][:, dst * NE:(dst + 1) * NE], ones, sel[:, 0, :], start=True, stop=False)
                last = mm(ps[5][:, dst * NE:(dst + 1) * NE], m, sel[:, 1, :], start=False, stop=True)
            last.then_inc(pos_mm, 1)

            pe.wait_ge(tab_done, 1)
            runs = pe.value_load(tab[0:1, 0:1], min_val=NE, max_val=NE + V_EXTRA)
            pe.wait_ge(m_cs, 1)
            for n in range(2):
                last = mm(ps[4 + n][:, :], cmb[:, 0:P], tn[:, 0, n * 512:(n + 1) * 512], start=True, stop=True)
            last.then_inc(m_zero, 1)

            def gather():
                for g in range(2):
                    for cc in range(4):
                        c = 4 * g + cc
                        for t in range(T):
                            last = mm(ps[7 - g][:, cc * P:(cc + 1) * P], tn[:, t, c * P:(c + 1) * P], pick[:, t, :],
                                      start=t == 0, stop=t == T - 1)
                    last.then_inc(m_gat, 1)
                    yield

            def combine(v):
                pe.wait_ge(m_ye, v + 1)
                pe.wait_ge(m_cs, v + 1)
                for i in range(4):
                    n, t = i // 2, i % 2
                    if i >= 2:
                        pe.wait_ge(m_add, v * 4 + (i - 1))
                    mm(ps[6 + i % 2][:, :], cmb[:, t * P:(t + 1) * P], ye[:, n * 512:(n + 1) * 512],
                       start=True, stop=True).then_inc(m_cmb, 1)

            pe.wait_ge(m_pick, 2)
            for _ in gather():
                pass

            with pe.Fori(0, runs) as v:
                def eup(k, bank, c, h):
                    ready(U_MOE + k, v, U_RUN)
                    wh, wl = moe_slot(k)
                    for cc in range(4):
                        cd = 4 * h + cc
                        last = mm3(ps[bank + c % 2][:, :], hth[:, cd, 0:P], htl[:, cd, 0:P],
                                   wh[:, cc * EW:(cc + 1) * EW], wl[:, cc * EW:(cc + 1) * EW], cd == 0, cd == DC - 1)
                    last.then_inc(unit_used, 1)

                def edown(k, c):
                    pe.wait_ge(m_gl, v * ESTEPS + (c + 1))
                    for n in range(2):
                        ready(U_MOE + k + n, v, U_RUN)
                        wh, wl = moe_slot(k + n)
                        for f in range(4):
                            last = mm3(ps[4 + n][:, :], gth[:, f * P:(f + 1) * P], gtl[:, f * P:(f + 1) * P],
                                       wh[:, f * 512:(f + 1) * 512], wl[:, f * 512:(f + 1) * 512],
                                       c == 0 and f == 0, c == ESTEPS - 1 and f == 3)
                        last.then_inc(unit_used, 1)

                def eturn(c):
                    pe.wait_ge(m_g, v * ESTEPS + (c + 1))
                    for f in range(4):
                        last = tr(ps[6 + c % 2][:, f * P:(f + 1) * P], mg[:, f * P:(f + 1) * P])
                    last.then_inc(m_t, 1)

                pe.wait_ge(m_hl, v * 2 + 2)
                k = 0
                for c in range(ESTEPS):
                    eup(k, 0, c, 0)
                    eup(k + 1, 0, c, 1)
                    if c == 0:
                        combine(v)
                    else:
                        if c == 1:
                            pe.wait_ge(m_add, v * 4 + 4)
                        eturn(c - 1)
                    eup(k + 2, 2, c, 0)
                    eup(k + 3, 2, c, 1)
                    k += 4
                    if c:
                        edown(k, c - 1)
                        k += 2
                eturn(ESTEPS - 1)
                pe.wait_ge(m_pick, v * 4 + 6)
                for t in range(T):
                    last = tr(ps[1][:, t * P:(t + 1) * P], gpick[:, t, :])
                last.then_inc(m_c, 1)
                halves = gather()
                next(halves)
                pe.wait_ge(m_gl, v * ESTEPS + ESTEPS)
                next(halves)
                edown(k, ESTEPS - 1)
            pe.wait_ge(m_hl, runs * 2 + 2)
            combine(runs)


_ORDER = ["x", "attn_norm", "ffn_norm", "a_w_dq", "a_g_cq", "a_w_uq", "a_w_dkv", "a_g_ckv", "a_w_ukv", "a_g_qn",
          "a_g_kn", "a_w_o", "kv_norm", "kv_w_k", "kv_w_v", "kv_g_kn", "b_w_q", "b_g_qn", "b_rel_bias", "b_w_o",
          "ffn_w1", "ffn_w3", "ffn_w2", "moe_router", "moe_w1", "moe_w3", "moe_w2"]


def _constants():
    import numpy as np

    c = np.zeros((P, C_ALL), np.float32)
    c[:, C_ID:C_ID + P] = np.eye(P)
    c[:, C_TRI:C_TRI + P] = np.triu(np.ones((P, P)), 1)
    c[:, C_IOTA:C_IOTA + P] = np.arange(P)
    c[:, C_ONES:C_ONES + P] = 1
    inv = np.float32(10000.0) ** (-np.arange(HALF, dtype=np.float32) / np.float32(HALF))
    angle = (np.arange(SEQ, dtype=np.float32)[:, None] * inv[None, :]).astype(np.float32)
    cos, sin = (f(angle.astype(np.float64)).reshape(T, P, HALF).transpose(1, 0, 2) for f in (np.cos, np.sin))
    c[:, C_ROPC:C_ROPC + T * ROPE] = np.concatenate([cos, cos], -1).reshape(P, -1)
    c[:, C_ROPS:C_ROPS + T * ROPE] = np.concatenate([-sin, sin], -1).reshape(P, -1)
    c[:, C_REV:C_REV + T * NE] = np.tile(NE - np.arange(NE), T)
    c[0, C_MA:C_MA + CHUNK] = 1
    c[0, C_MB:C_MB + CHUNK] = MASKED
    return c


def kernel(**inputs):
    import numpy as np
    import concourse.bacc as bacc
    from concourse.bass_utils import run_bass_kernel_spmd

    nc = bacc.Bacc("TRN2", target_bir_lowering=False, num_devices=1)
    arrays, args = {}, []
    for name in _ORDER:
        a = np.ascontiguousarray(inputs[name])
        if name == "b_rel_bias":
            reach = (a.shape[2] - 1) // 2
            a = np.ascontiguousarray(a[0][:, np.clip(SEQ - 1 - np.arange(SPAN), -reach, reach) + reach])
        if a.ndim == 1:
            a = a.reshape(1, -1)
        arrays[f"in_{name}"] = a
        args.append(nc.dram_tensor(f"in_{name}", a.shape, mybir.dt.from_np(a.dtype), kind="ExternalInput").ap())
    consts = _constants()
    arrays["in_consts"] = consts
    args.append(nc.dram_tensor("in_consts", consts.shape, mybir.dt.float32, kind="ExternalInput").ap())
    args.append(nc.dram_tensor("out_0", (1, SEQ, D), mybir.dt.float32, kind="ExternalOutput").ap())
    trunk_kernel(nc, *args)
    r = run_bass_kernel_spmd(nc, [arrays], core_ids=[0])
    return r.results[0]["out_0"]
```

```python
import concourse.bass as bass
from concourse import mybir
from contextlib import ExitStack

P = 128
D = 1024
SEQ = 256
T = SEQ // P
DC = D // P
CHUNK = 64
HEADS = 16
PAIRS = HEADS // 2
NOPE, ROPE, VDIM = 64, 32, 64
QK = NOPE + ROPE
HALF = ROPE // 2
Q_LORA, KV_LORA = 384, 256
QC, KVC = Q_LORA // P, KV_LORA // P
HD = D // HEADS
FF = 2816
FW = 256
FSTEPS = FF // FW
NE = 8
EFF = 3584
EW = 512
ESTEPS = EFF // EW
EPS = 1e-6
SPAN = P + SEQ
UNIT = 2048
RAW = 6
SPLIT = 3

U_DQ, U_DKV, U_UQ, U_UKV, U_WO0 = 0, 2, 4, 7, 9
U_FFN = 13
U_L1 = U_FFN + 3 * FSTEPS
U_MOE = U_L1 + 16
U_RUN = 6 * ESTEPS
V_EXTRA = 3

C_ID, C_TRI, C_IOTA, C_ONES, C_ROPC, C_ROPS, C_REV, C_MA, C_MB = 0, 128, 256, 384, 512, 576, 640, 656, 784
C_BEF = C_MB + CHUNK
C_I3 = C_BEF + NE * NE
C_E3 = C_I3 + V_EXTRA * NE
C_ALL = C_E3 + V_EXTRA * NE
MASKED = -2.0 ** 100

G_ATT, G_FFN, G_KV, G_CQ, G_CKV = 0, 16, 32, 40, 43
G_ALL = 45


def width(n):
    if n < U_DKV:
        return 4 * Q_LORA
    if n < U_UQ:
        return 4 * (KV_LORA + ROPE)
    if n < U_UKV:
        return QC * 512
    return UNIT


def trunk_kernel(nc, x, attn_norm, ffn_norm, w_dq, g_cq, w_uq, w_dkv, g_ckv, w_ukv, g_qn, g_kn, w_oa,
                 kv_norm, w_k, w_v, g_kk, w_q, g_qq, bias_rows, w_ob, w1, w3, w2, router, mw1, mw3, mw2,
                 consts, out):
    fp32, f32r, i32 = mybir.dt.float32, mybir.dt.float32r, mybir.dt.int32
    ALU = mybir.AluOpType
    ACT = mybir.ActivationFunctionType
    AX = mybir.AxisListType.X
    ds = bass.ds

    bias_wide = nc.dram_tensor("bias_wide", (HEADS, P, SPAN), fp32, kind="Internal").ap()

    x_v = x.rearrange("b (t p) d -> p (b t) d", p=P)
    out_v = out.rearrange("b (t p) d -> p (b t) d", p=P)

    def rows(w):
        return w.rearrange("(c p) n -> p c n", p=P)

    dq_v, uq_v, dkv_v, ukv_v, oa_v = (rows(w.rearrange("a d n -> (a d) n")) for w in (w_dq, w_uq, w_dkv, w_ukv, w_oa))
    l1_v = [rows(w_q.rearrange("a d n -> (a d) n")), rows(w_k), rows(w_v), rows(w_ob.rearrange("a d n -> (a d) n"))]
    w1_v, w3_v, w2_v = (rows(w.rearrange("a d n -> (a d) n")) for w in (w1, w3, w2))
    m1_v, m3_v, m2_v = (rows(w.rearrange("a e d n -> (a e d) n")) for w in (mw1, mw3, mw2))
    rt_v = rows(router.rearrange("a d n -> (a d) n"))

    ctx = ExitStack()
    with ctx:
        def sem(name):
            return ctx.enter_context(nc.semaphore(name))

        def sb(name, shape, dt=fp32, at=ctx):
            return at.enter_context(nc.sbuf_tensor(name, shape, dt))

        xr = sb("xr", [P, T, D])
        tn = sb("tn", [P, T, D])
        hth = sb("hth", [P, DC, SEQ], f32r)
        htl = sb("htl", [P, DC, SEQ], f32r)
        raw = sb("raw", [P, RAW, UNIT])
        wh_a = sb("wh_a", [P, SPLIT, UNIT], f32r)
        wl_a = sb("wl_a", [P, SPLIT, UNIT], f32r)
        cst = sb("cst", [P, C_ALL])
        grow = sb("grow", [G_ALL, P])
        gcol = sb("gcol", [P, G_ALL])
        qkg = sb("qkg", [P, 2, 2])
        pe_g = sb("pe_g", [P, 2, 2, ROPE])
        ropt = sb("ropt", [P, 2, 2, T, ROPE])
        mask = sb("mask", [P, P + CHUNK], f32r)
        negh = sb("negh", [P, T])
        ss = sb("ss", [P, 6])
        rstd = sb("rstd", [P, 4])
        ssh = sb("ssh", [P, 2, T, HEADS])
        rsh = sb("rsh", [P, 2, T, HEADS])
        rtmp = sb("rtmp", [P, 2 * T * HEADS])
        nmax = sb("nmax", [P, 2, T, 2])
        rsum = sb("rsum", [P, 2, T, 2])
        rinv = sb("rinv", [P, 2, T, 2])
        wr = sb("wr", [P, DC, NE])
        wrs = sb("wrs", [P, DC, 2 * NE], f32r)
        lgt = sb("lgt", [2 * NE, SEQ])

        lg = sb("lg", [P, T, NE])
        work = sb("work", [P, 8, T, NE])
        tops = sb("tops", [P, 8, T])
        over = sb("over", [P, 3, NE])
        prior = sb("prior", [P, NE, NE])
        hot = sb("hot", [P, V_EXTRA, NE])
        hot_t = sb("hot_t", [P, V_EXTRA, T, NE])
        pos_v = sb("pos_v", [P, NE + V_EXTRA + 1, T])
        gate_v = sb("gate_v", [P, NE + V_EXTRA + 1, T])
        tabf = sb("tabf", [P, 8])
        tab = sb("tab", [P, 8], i32)
        kpr = sb("kpr", [P, T, ROPE])

        pre = ExitStack()
        q_all = sb("q_all", [P, T, HEADS * QK], at=pre)
        kv_all = sb("kv_all", [P, T, 2 * D], at=pre)
        att = ExitStack()
        prob = sb("prob", [P, 2, 2, SPAN], at=att)
        probT = sb("probT", [P, 2, 2, SPAN], at=att)
        att.enter_context(nc.sbuf_tensor("att_gap", [P, 2 * DC * SEQ - 8 * SPAN], fp32))
        bias = sb("bias", [P, 2, 2, SPAN], at=att)
        qn = sb("qn", [P, 2, T, 2 * QK], at=att)
        kn = sb("kn", [P, 2, T, 2 * QK], at=att)
        qT = sb("qT", [P, 2, 2 * SEQ], at=att)
        kT = sb("kT", [P, 2, 2 * SEQ], at=att)
        att.close()
        sq = ExitStack()
        squares = sb("squares", [P, T * HEADS * QK], at=sq)
        roptmp = sb("roptmp", [P, T, 2, HEADS, ROPE], at=sq)
        kpsq = sb("kpsq", [P, T, ROPE], at=sq)
        kpe = sb("kpe", [P, T, ROPE], at=sq)
        ch = sb("ch", [P, QC + KVC, SEQ], f32r, at=sq)
        cl = sb("cl", [P, QC + KVC, SEQ], f32r, at=sq)
        sq.close()
        l1 = ExitStack()
        h2h = sb("h2h", [P, DC, SEQ], f32r, at=l1)
        h2l = sb("h2l", [P, DC, SEQ], f32r, at=l1)
        squares1 = sb("squares1", [P, T * D], at=l1)
        l1.close()
        ffn = ExitStack()
        fs = sb("fs", [P, 2, 2 * SEQ], at=ffn)
        fg = sb("fg", [P, 2, 2 * SEQ], at=ffn)
        fgh = sb("fgh", [P, 2, 2 * SEQ], f32r, at=ffn)
        fgl = sb("fgl", [P, 2, 2 * SEQ], f32r, at=ffn)
        ffn.close()
        pre.close()
        moe = ctx.enter_context(ExitStack())
        wh_b = sb("wh_b", [P, SPLIT, UNIT], f32r, at=moe)
        wl_b = sb("wl_b", [P, SPLIT, UNIT], f32r, at=moe)
        ms = sb("ms", [P, 2, EW], at=moe)
        mg = sb("mg", [P, EW], at=moe)
        gth = sb("gth", [P, EW], f32r, at=moe)
        gtl = sb("gtl", [P, EW], f32r, at=moe)
        ye = sb("ye", [P, D], at=moe)
        cmb = sb("cmb", [P, SEQ], at=moe)
        pick = sb("pick", [P, T, P], at=moe)
        gpick = sb("gpick", [P, T, P], at=moe)
        cur = sb("cur", [P, 3, T], at=moe)
        ps = [ctx.enter_context(nc.psum_tensor(f"ps{i}", [P, 512], fp32)) for i in range(8)]

        ident = cst[:, C_ID:C_ID + P]
        tri = cst[:, C_TRI:C_TRI + P]
        iota = cst[:, C_IOTA:C_IOTA + P]
        ones = cst[:, C_ONES:C_ONES + P]
        ropc = cst[:, C_ROPC:C_ROPC + T * ROPE].rearrange("p (t r) -> p t r", t=T)
        rops = cst[:, C_ROPS:C_ROPS + T * ROPE].rearrange("p (t r) -> p t r", t=T)
        rev = cst[:, C_REV:C_REV + T * NE].rearrange("p (t e) -> p t e", t=T)
        before = cst[:, C_BEF:C_BEF + NE * NE].rearrange("p (a e) -> p a e", e=NE)
        nth = cst[:, C_I3:C_I3 + V_EXTRA * NE].rearrange("p (i e) -> p i e", e=NE)
        number = cst[:, C_E3:C_E3 + V_EXTRA * NE].rearrange("p (i e) -> p i e", e=NE)
        mask_row = mask[:, 0:P]
        mask_col = mask[:, P:P + CHUNK]

        q1 = q_all[:, :, 0:D]
        k1 = kv_all[:, :, 0:D]
        v1 = kv_all[:, :, D:2 * D]

        def heads(a, w, lo=0, hi=None):
            return a.rearrange("p t (h w) -> p t h w", w=w)[:, :, :, lo:w if hi is None else hi]

        raw_here = [sem(f"raw_here{i}") for i in range(RAW)]
        hi_done = sem("hi_done")
        lo_done = sem("lo_done")
        unit_used = sem("unit_used")
        x_here = sem("x_here")
        c_here = sem("c_here")
        mask_done = sem("mask_done")
        g_here = sem("g_here")
        hg_here = sem("hg_here")
        wr_here = sem("wr_here")
        gcol_tr = sem("gcol_tr")
        gcol_done = sem("gcol_done")
        pool_init = sem("pool_init")
        rope_tab = sem("rope_tab")
        ss_done = sem("ss_done")
        ss_lat = sem("ss_lat")
        p_step = sem("p_step")
        rstd_done = sem("rstd_done")
        rstd_lat = sem("rstd_lat")
        tn_done = sem("tn_done")
        tr_done = sem("tr_done")
        th_done = sem("th_done")
        tl_done = sem("tl_done")
        h2_hi = sem("h2_hi")
        h2_done = sem("h2_done")
        xr_done = sem("xr_done")
        y_done = [sem(f"y_done{i}") for i in range(3)]
        lat_tn = sem("lat_tn")
        lat_tr = sem("lat_tr")
        lat_h = sem("lat_h")
        lat_l = sem("lat_l")
        pj_a = [sem("pj_a0"), sem("pj_a1")]
        pj_v = [sem("pj_v0"), sem("pj_v1")]
        sq_done = [sem("sq_done0"), sem("sq_done1")]
        sh_done = [sem("sh_done0"), sem("sh_done1")]
        var_done = [sem("var_done0"), sem("var_done1")]
        std_done = [sem("std_done0"), sem("std_done1")]
        zeroed = sem("zeroed")
        kps_done = sem("kps_done")
        rs_done = [sem("rs_done0"), sem("rs_done1")]
        rq_done = sem("rq_done")
        rk_done = sem("rk_done")
        A = []
        for la in range(2):
            A.append({k: sem(f"{k}_{la}") for k in (
                "qn", "kn",
                "tq", "tk",
                "qT", "kT",
                "s",
                "sb",
                "nm",
                "ex",
                "pt",
                "pa", "pv",
                "o",
                "ri",
                "oo")})
        wide_done = sem("wide_done")
        bias_here = [sem("bias_here0"), sem("bias_here1")]
        v_step = sem("v_step")
        f_s = sem("f_s")
        f_g = sem("f_g")
        f_gh = sem("f_gh")
        f_gl = sem("f_gl")
        wrh_done = sem("wrh_done")
        wrl_done = sem("wrl_done")
        lg_mm = sem("lg_mm")
        lg_out = sem("lg_out")
        lg_tr = sem("lg_tr")
        v_done = sem("v_done")
        e_done = sem("e_done")
        sel_done = sem("sel_done")
        pos_mm = sem("pos_mm")
        tab_done = sem("tab_done")
        m_zero = sem("m_zero")
        m_s = sem("m_s")
        m_g = sem("m_g")
        m_t = sem("m_t")
        m_gh = sem("m_gh")
        m_gl = sem("m_gl")
        m_ye = sem("m_ye")
        m_gat = sem("m_gat")
        m_hh = sem("m_hh")
        m_hl = sem("m_hl")
        m_cur = sem("m_cur")
        m_pick = sem("m_pick")
        m_c = sem("m_c")
        m_cs = sem("m_cs")
        m_cmb = sem("m_cmb")
        m_add = sem("m_add")
        out_done = sem("out_done")

        TURN_BANKS = DC // 2
        TURN = {"n0": 0, "a0": 1, "n1": 2, "n2": 3, "a1": 4, "n3": 5}

        def split_slot(n):
            return wh_a[:, n % SPLIT, :], wl_a[:, n % SPLIT, :]

        def moe_slot(k):
            s = k % (2 * SPLIT)
            h, l = (wh_a, wl_a) if s < SPLIT else (wh_b, wl_b)
            return h[:, s % SPLIT, :], l[:, s % SPLIT, :]

        def latent_out(i):
            if i < 6:
                return U_UQ + i // 2 + 1, q_all[:, i % 2, (i // 2) * 512:(i // 2 + 1) * 512]
            k = (i - 6) // 2
            return U_UKV + (i - 6) // 4 + 1, kv_all[:, i % 2, k * 512:(k + 1) * 512]

        def q_rope(t):
            return heads(q_all[:, t:t + 1, :], QK, NOPE)[:, 0]

        def rotate(engine, t):
            def fac(s, a, b):
                return ropt[:, 0, s, t:t + 1, a:b].to_broadcast([P, HEADS, b - a])

            qp = q_rope(t)
            engine.tensor_tensor(roptmp[:, t, 0], qp, fac(0, 0, ROPE), ALU.mult)
            engine.tensor_tensor(roptmp[:, t, 1, :, 0:HALF], qp[:, :, HALF:ROPE], fac(1, 0, HALF), ALU.mult)
            return engine.tensor_tensor(roptmp[:, t, 1, :, HALF:ROPE], qp[:, :, 0:HALF], fac(1, HALF, ROPE), ALU.mult)

        block = ctx.enter_context(nc.Block())

        @block.sync
        def _(sp):
            for t in range(T):
                sp.dma_start(xr[:, t, :], x_v[:, t, :]).then_inc(x_here, 16)

            def load(n, src, shape, j=0, j_units=0, slot_n=None):
                a, b = shape
                dst = raw[:, n % RAW, 0:a * b].rearrange("p (a b) -> p a b", a=a)
                if n >= RAW:
                    sp.wait_ge(lo_done, n - RAW + 1 + j * j_units)
                sp.dma_start(dst, src).then_inc(raw_here[n % RAW], 16)

            for h in range(2):
                load(U_DQ + h, dq_v[:, 4 * h:4 * h + 4, :], (4, Q_LORA))
            for h in range(2):
                load(U_DKV + h, dkv_v[:, 4 * h:4 * h + 4, :], (4, KV_LORA + ROPE))
            for n in range(3):
                load(U_UQ + n, uq_v[:, :, n * 512:(n + 1) * 512], (QC, 512))
            for n in range(2):
                load(U_UKV + n, ukv_v[:, :, n * 1024:(n + 1) * 1024], (KVC, 1024))
            for n in range(2):
                for h in range(2):
                    load(U_WO0 + 2 * n + h, oa_v[:, 4 * h:4 * h + 4, n * 512:(n + 1) * 512], (4, 512))
            for w, v in enumerate((w1_v, w3_v)):
                load(U_FFN + w, v[:, :, 0:FW], (DC, FW))
            with sp.Fori(0, (FSTEPS - 1) // 2) as j:
                for u in range(2):
                    n = U_FFN + 2 + 3 * u
                    for w, v in enumerate((w1_v, w3_v)):
                        load(n + w, v[:, :, ds(j * (2 * FW) + (1 + u) * FW, FW)], (DC, FW), j, 6)
                    load(n + 2, w2_v[:, ds(j * 4 + 2 * u, 2), :], (2, D), j, 6)
            load(U_L1 - 1, w2_v[:, 2 * (FSTEPS - 1):2 * FSTEPS, :], (2, D))
            for w in range(4):
                for n in range(2):
                    for h in range(2):
                        load(U_L1 + 4 * w + 2 * n + h, l1_v[w][:, 4 * h:4 * h + 4, n * 512:(n + 1) * 512], (4, 512))

            def expert(e, j):
                k = 0
                for c in range(ESTEPS + 1):
                    if c < ESTEPS:
                        for v in (m1_v, m3_v):
                            for h in range(2):
                                load(U_MOE + k, v[:, ds(e * DC + 4 * h, 4), c * EW:(c + 1) * EW], (4, EW), j, U_RUN)
                                k += 1
                    if c:
                        for n in range(2):
                            load(U_MOE + k, m2_v[:, ds(e * (EFF // P) + 4 * (c - 1), 4), n * 512:(n + 1) * 512],
                                 (4, 512), j, U_RUN)
                            k += 1
                assert k == U_RUN

            with sp.Fori(0, NE) as e:
                expert(e, e)
            sp.wait_ge(tab_done, 1)
            extra = sp.value_load(tab[0:1, 1:2], min_val=0, max_val=V_EXTRA)
            with sp.If(extra > 0):
                with sp.Fori(0, extra) as i:
                    e = sp.value_load(tab[0:1, ds(i + 2, 1)], min_val=0, max_val=NE - 1)
                    expert(e, i + NE)
            runs = sp.value_load(tab[0:1, 0:1], min_val=NE, max_val=NE + V_EXTRA)
            sp.wait_ge(m_add, runs * 4 + 4)
            for t in range(T):
                sp.dma_start(out_v[:, t, :], xr[:, t, :]).then_inc(out_done, 16)
            sp.wait_ge(out_done, 16 * T)

        @block.gpsimd
        def _(pool):
            steps = [0]

            def chain(ins):
                steps[0] += 1
                ins.then_inc(p_step, 1)
                pool.wait_ge(p_step, steps[0])

            nc.gpsimd.memset(negh[:], -0.5).then_inc(pool_init, 1)
            nc.gpsimd.memset(qkg[:, 0, :], 1.0).then_inc(pool_init, 1)
            pool.wait_ge(pool_init, 2)

            def root(dst, src, n):
                chain(nc.gpsimd.tensor_scalar(dst, src, 1.0 / n, EPS, ALU.mult, ALU.add))
                return nc.gpsimd.tensor_tensor(dst, dst, negh[:, 0:dst.shape[1]], ALU.pow)

            def norm(m):
                for t in range(T):
                    pool.wait_ge(ss_done, T * m + t + 1)
                    root(rstd[:, t:t + 1], ss[:, t:t + 1], D).then_inc(rstd_done, 1)

            norm(0)
            with nc.allow_non_contiguous_dma("a few gains"):
                for i, g in enumerate((g_qn, g_kn)):
                    pool.dma_start(qkg[0:NOPE, 0, i:i + 1], g[0:1, 0:NOPE].rearrange("a p -> p a")).then_inc(hg_here, 16)
                for i, g in enumerate((g_qq, g_kk)):
                    for h in range(2):
                        pool.dma_start(qkg[h * HD:(h + 1) * HD, 1, i:i + 1], g.rearrange("a p -> p a")).then_inc(hg_here, 16)
            for i, g in enumerate((g_qn, g_kn)):
                for s, parts in enumerate((((0, NOPE, ROPE),), ((0, NOPE + HALF, HALF), (HALF, NOPE, HALF)))):
                    for at, src, n in parts:
                        pool.dma_start(pe_g[:, i, s, at:at + n],
                                       g[0:1, src:src + n].to_broadcast([P, n])).then_inc(hg_here, 16)
            pool.wait_ge(hg_here, 16 * 12)
            pool.wait_ge(c_here, 16)
            for i in range(2):
                for s, tab_ in enumerate((ropc, rops)):
                    chain(nc.gpsimd.tensor_tensor(ropt[:, i, s, :, :], tab_,
                                                  pe_g[:, i, s:s + 1, :].to_broadcast([P, T, ROPE]), ALU.mult))
            chain(nc.gpsimd.tensor_scalar(ropt[:, 0, :, :, :], ropt[:, 0, :, :, :], QK ** -0.5, None, ALU.mult))
            nc.gpsimd.tensor_scalar(qkg[0:NOPE, 0, 0:1], qkg[0:NOPE, 0, 0:1], QK ** -0.5, None, ALU.mult).then_inc(rope_tab, 1)
            nc.gpsimd.tensor_scalar(qkg[:, 1, 0:1], qkg[:, 1, 0:1], HD ** -0.5, None, ALU.mult).then_inc(rope_tab, 1)

            pool.wait_ge(ss_lat, 2)
            root(rstd[:, 0:T], ss[:, 0:T], Q_LORA).then_inc(rstd_lat, 1)
            pool.wait_ge(ss_lat, 4)
            root(rstd[:, T:2 * T], ss[:, T:2 * T], KV_LORA).then_inc(rstd_lat, 1)
            pool.wait_ge(lat_tn, 4)
            ka, kb = roptmp[:, 1, 0, 0:T, :], roptmp[:, 1, 1, 0:T, :]
            nc.gpsimd.tensor_tensor(ka, kpe[:], ropt[:, 1, 0], ALU.mult)
            nc.gpsimd.tensor_tensor(kb[:, :, 0:HALF], kpe[:, :, HALF:ROPE], ropt[:, 1, 1, :, 0:HALF], ALU.mult)
            chain(nc.gpsimd.tensor_tensor(kb[:, :, HALF:ROPE], kpe[:, :, 0:HALF], ropt[:, 1, 1, :, HALF:ROPE], ALU.mult))
            nc.gpsimd.tensor_tensor(kpr[:], ka, kb, ALU.add).then_inc(rk_done, 1)
            pool.wait_ge(rk_done, 1)
            pool.wait_ge(sq_done[0], 2)
            chain(rotate(nc.gpsimd, 1))
            nc.gpsimd.tensor_tensor(q_rope(1), roptmp[:, 1, 0], roptmp[:, 1, 1], ALU.add).then_inc(rq_done, 1)

            def scale_k(la, p, par, first=False):
                if not first:
                    pool.wait_ge(A[la]["tk"], p - 1)
                if la == 0:
                    dst = kn[:, par].rearrange("p t (h w) -> p t h w", h=2)
                    r = rsh[:, 1, :, ds(p * 2, 2)].unsqueeze(3)
                    src = kv_all[:].rearrange("p t (h w) -> p t h w", h=HEADS)[:, :, ds(p * 2, 2), 0:NOPE]
                    nc.gpsimd.tensor_tensor(dst[:, :, :, 0:NOPE], src, r.to_broadcast([P, T, 2, NOPE]), ALU.mult)
                    nc.gpsimd.tensor_tensor(dst[:, :, :, NOPE:QK], kpr[:].unsqueeze(2).to_broadcast([P, T, 2, ROPE]),
                                            r.to_broadcast([P, T, 2, ROPE]), ALU.mult).then_inc(A[la]["kn"], 1)
                else:
                    dst = kn[:, par, :, 0:2 * HD].rearrange("p t (h w) -> p t h w", h=2)
                    r = rsh[:, 1, :, ds(p * 2, 2)].unsqueeze(3)
                    src = k1.rearrange("p t (h w) -> p t h w", h=HEADS)[:, :, ds(p * 2, 2), :]
                    nc.gpsimd.tensor_tensor(dst, src, r.to_broadcast([P, T, 2, HD]), ALU.mult).then_inc(A[la]["kn"], 1)

            def attention(la):
                scale_k(la, 0, 0, first=True)
                scale_k(la, 1, 1, first=True)
                with pool.Fori(0, PAIRS // 2 - 1) as j:
                    for u in range(2):
                        scale_k(la, j * 2 + (2 + u), u)

            pool.wait_ge(rs_done[0], 1)
            attention(0)
            pool.wait_ge(A[0]["s"], HEADS)
            nc.gpsimd.memset(kT[HD:P, :, 0:SEQ], 0.0).then_inc(zeroed, 1)
            pool.wait_ge(zeroed, 1)
            nc.gpsimd.memset(kT[0:HD, :, SEQ:2 * SEQ], 0.0).then_inc(zeroed, 1)
            pool.wait_ge(zeroed, 2)
            norm(1)
            norm(2)
            pool.wait_ge(rs_done[1], 1)
            attention(1)
            norm(3)

        @block.scalar
        def _(act):
            act.dma_start(cst[:], consts).then_inc(c_here, 16)
            for at, g, n in ((G_ATT, attn_norm, 2 * DC), (G_FFN, ffn_norm, 2 * DC), (G_CQ, g_cq, QC), (G_CKV, g_ckv, KVC)):
                act.dma_start(grow[at:at + n, :], g.rearrange("l (c p) -> (l c) p", p=P)).then_inc(g_here, 16)
            act.dma_start(grow[G_KV:G_KV + DC, :], kv_norm.rearrange("a (c p) -> (a c) p", p=P)).then_inc(g_here, 16)

            def hi(n, j=0, j_units=0, w=None):
                moe_unit = n - U_MOE
                dst = moe_slot(moe_unit)[0] if moe_unit >= 0 else split_slot(n)[0]
                w = width(n) if w is None else w
                act.wait_ge(raw_here[n % RAW], 16 * (n // RAW + 1) + j * (16 * j_units // RAW))
                if moe_unit >= 0:
                    act.wait_ge(unit_used, n - 2 * SPLIT + 1 + j * j_units)
                elif n >= SPLIT:
                    act.wait_ge(unit_used, n - SPLIT + 1 + j * j_units)
                nc.scalar.activation(dst[:, 0:w], raw[:, n % RAW, 0:w], ACT.Copy).then_inc(hi_done, 1)

            def sum_squares(m, first):
                for t in range(T):
                    if first:
                        act.wait_ge(x_here, 16 * T)
                    else:
                        act.wait_ge(xr_done, 4 * (m - 1) + 3 + t)
                    nc.scalar.activation(tn[:, t, :], xr[:, t, :], ACT.Square, accum_out=ss[:, t:t + 1]).then_inc(ss_done, 1)

            def turn_out(name, dsts):
                k = TURN[name]
                for b in range(TURN_BANKS):
                    act.wait_ge(tr_done, TURN_BANKS * k + b + 1)
                    for cc in range(2):
                        c = 2 * b + cc
                        for dst, g in dsts:
                            kw = {} if g is None else {"scale": gcol[:, g + c:g + c + 1]}
                            last = nc.scalar.activation(dst[:, c, :], ps[b][:, cc * SEQ:(cc + 1) * SEQ], ACT.Copy, **kw)
                    last.then_inc(th_done, 1)

            sum_squares(0, True)
            act.wait_ge(c_here, 16)
            nc.scalar.activation(mask[:], cst[:, C_MA:C_MA + P + CHUNK], ACT.Copy).then_inc(mask_done, 1)
            hi(0)
            hi(1)
            act.wait_ge(gcol_done, 1)
            turn_out("n0", [(hth, G_ATT)])
            hi(2)
            hi(3)
            act.dma_start(wr[:], rt_v).then_inc(wr_here, 16)
            act.wait_ge(unit_used, U_DKV)
            for t in range(T):
                nc.scalar.activation(squares[:, t * Q_LORA:(t + 1) * Q_LORA], ps[4 + t][:, 0:Q_LORA], ACT.Square,
                                     accum_out=ss[:, t:t + 1]).then_inc(ss_lat, 1)
            hi(4)
            hi(5)
            act.wait_ge(unit_used, U_UQ)
            for t in range(T):
                nc.scalar.activation(squares[:, T * Q_LORA + t * KV_LORA:T * Q_LORA + (t + 1) * KV_LORA], ps[6 + t][:, 0:KV_LORA], ACT.Square,
                                     accum_out=ss[:, T + t:T + t + 1]).then_inc(ss_lat, 1)
            for b in range(3):
                act.wait_ge(lat_tr, b + 1)
                for cc in range(2 if b < 2 else 1):
                    c = 2 * b + cc
                    last = nc.scalar.activation(ch[:, c, :], ps[b][:, cc * SEQ:(cc + 1) * SEQ], ACT.Copy,
                                                scale=gcol[:, G_CQ + c:G_CQ + c + 1])
                last.then_inc(lat_h, 1)
            act.wait_ge(lat_tn, 4)
            for t in range(T):
                nc.scalar.activation(kpsq[:, t, :], kpe[:, t, :], ACT.Square, accum_out=ss[:, 4 + t:5 + t]).then_inc(kps_done, 1)

            def k_squares(h):
                for t in range(T):
                    act.wait_ge(sh_done[0], 2 if h and t else 1)
                    at = (2 * t + h) * HEADS * NOPE // 2
                    nc.scalar.activation(squares[:, at:at + HEADS * NOPE // 2].rearrange("p (h w) -> p h w", w=NOPE),
                                         heads(kv_all[:, t:t + 1, :], NOPE + VDIM, 0, NOPE)[:, 0, h * HEADS // 2:(h + 1) * HEADS // 2],
                                         ACT.Square).then_inc(sq_done[0], 1)

            for i in range(14):
                if i % 2 == 0:
                    act.wait_ge(unit_used, latent_out(i)[0])
                    nc.scalar.activation(latent_out(i)[1], ps[4 + i % 4][:, :], ACT.Copy).then_inc(pj_a[0], 1)
                if i in (1, 3, 5, 9):
                    hi({1: 6, 3: 7, 5: 8, 9: 9}[i])
                if i == 6:
                    act.wait_ge(pj_a[0], 3)
                    act.wait_ge(pj_v[0], 3)
                    for t in range(T):
                        nc.scalar.activation(squares[:, t * HEADS * QK:(t + 1) * HEADS * QK], q_all[:, t, :], ACT.Square).then_inc(sq_done[0], 1)
                if i == 11:
                    act.wait_ge(pj_a[0], 5)
                    act.wait_ge(pj_v[0], 5)
                    k_squares(0)
            act.wait_ge(pj_a[0], 7)
            act.wait_ge(pj_v[0], 7)
            k_squares(1)

            def head_std(la):
                act.wait_ge(var_done[la], 1)
                nc.scalar.activation(rsh[:].rearrange("p a t h -> p (a t h)"), ssh[:].rearrange("p a t h -> p (a t h)"),
                                     ACT.Sqrt).then_inc(std_done[la], 1)

            head_std(0)

            def attention(la):
                a = A[la]
                w = QK if la == 0 else P
                n = 2 * SEQ if la == 0 else SEQ

                def load_bias(p, par, wait=True):
                    if wait:
                        act.wait_ge(a["ex"], p * 2 - 2)
                    act.dma_start(bias[:, par, :, :], bias_wide[ds(p * 2, 2), :, :].rearrange("h q k -> q h k")).then_inc(bias_here[par], 16)

                def q_out(p, par):
                    act.wait_ge(a["tq"], p + 1)
                    nc.scalar.activation(qT[0:w, par, 0:n], ps[0][0:w, 0:n], ACT.Copy,
                                         scale=qkg[0:w, la, 0:1]).then_inc(a["qT"], 1)

                def probs(p, par, h):
                    act.wait_ge(a["nm"], p * 2 + (h + 1))
                    src = ps[2 + h] if la == 0 else bias[:, par, h, :]
                    for t, (lo_, n_) in enumerate(((0, P), (P, SEQ))):
                        last = nc.scalar.activation(prob[:, par, h, lo_:lo_ + n_], src[:, lo_:lo_ + n_], ACT.Exp,
                                                    bias=nmax[:, par, t, h:h + 1], accum_out=rsum[:, par, t, h:h + 1])
                    last.then_inc(a["ex"], 1)

                def pt_out(p, par):
                    act.wait_ge(a["pt"], p * 2 + 1)
                    nc.scalar.activation(probT[:, par, 0, :], ps[4][:, 0:SPAN], ACT.Copy).then_inc(a["pa"], 1)

                def step(p, par):
                    q_out(p + 1, 1 - par)
                    probs(p, par, 1)
                    pt_out(p, par)
                    probs(p + 1, 1 - par, 0)

                if la == 1:
                    act.wait_ge(wide_done, 32)
                    load_bias(0, 0, wait=False)
                    load_bias(1, 1, wait=False)
                q_out(0, 0)
                yield
                probs(0, 0, 0)
                with act.Fori(0, PAIRS // 2 - 1) as j:
                    for u in range(2):
                        step(j * 2 + u, u)
                        if la == 1:
                            load_bias(j * 2 + (u + 2), u, wait=True)
                step(PAIRS - 2, 0)
                probs(PAIRS - 1, 1, 1)
                pt_out(PAIRS - 1, 1)
                yield

            for at, skip, keys in ((0, P, P), (P, 0, SEQ)):
                src = bass.AP(tensor=bias_rows.tensor, offset=P - 1 + skip, ap=[[SPAN, HEADS], [-1, P], [1, keys]])
                act.dma_start(bias_wide[:, :, at:at + keys], src).then_inc(wide_done, 16)
            act.wait_ge(rope_tab, 2)
            for _ in attention(0):
                pass
            hi(U_WO0 + 1)
            turn_out("a0", [(hth, None)])
            for n in range(U_WO0 + 2, U_FFN + 2):
                hi(n)
            sum_squares(1, False)
            hi(U_FFN + 2)
            turn_out("n1", [(hth, G_FFN)])

            def f_silu(c, par):
                act.wait_ge(unit_used, U_FFN + 1 if isinstance(c, int) else c * 3 + U_FFN)
                nc.scalar.activation(fs[:, par, :], ps[par][:, :], ACT.Silu).then_inc(f_s, 1)

            def f_hi(c, par):
                act.wait_ge(f_g, c + 1)
                nc.scalar.activation(fgh[:, par, :], fg[:, par, :], ACT.Copy).then_inc(f_gh, 1)

            f_silu(0, 0)
            hi(U_FFN + 3)
            f_hi(0, 0)
            with act.Fori(0, (FSTEPS - 1) // 2) as j:
                for u in range(2):
                    n = U_FFN + 4 + 3 * u
                    hi(n, j, 6)
                    hi(n + 1, j, 6)
                    f_silu(j * 2 + (u + 1), 1 - u)
                    hi(n + 2, j, 6)
                    f_hi(j * 2 + (u + 1), 1 - u)
            hi(U_L1 + 1)
            sum_squares(2, False)
            turn_out("n2", [(hth, G_ATT + DC)])
            for c in range(DC):
                if c % 2 == 0:
                    act.wait_ge(tl_done, TURN_BANKS * TURN["n2"] + c // 2 + 1)
                last = nc.scalar.activation(h2h[:, c, :], ps[c // 2][:, c % 2 * SEQ:(c % 2 + 1) * SEQ], ACT.Copy,
                                            scale=gcol[:, G_KV + c:G_KV + c + 1])
                if c % 2:
                    last.then_inc(h2_hi, 1)
            for g in range(6):
                hi(U_L1 + 2 + 2 * g)
                hi(U_L1 + 3 + 2 * g)
                if g == 5:
                    att1 = attention(1)
                    next(att1)
                act.wait_ge(unit_used, U_L1 + 2 + 2 * g)
                nc.scalar.activation((q1, k1, v1)[g // 2][:, 0, (g % 2) * 512:(g % 2 + 1) * 512], ps[4 + g % 2 * 2][:, :],
                                     ACT.Copy).then_inc(pj_a[1], 1)
                if g in (1, 3):
                    act.wait_ge(pj_a[1], g + 1)
                    act.wait_ge(pj_v[1], g + 1)
                    if g == 3:
                        act.wait_ge(sh_done[1], 2)
                    for t in range(T):
                        nc.scalar.activation(squares1[:, t * D:(t + 1) * D], (q1, k1)[g // 2][:, t, :],
                                             ACT.Square).then_inc(sq_done[1], 1)
                if g == 3:
                    head_std(1)
            next(att1)
            hi(U_MOE - 2)
            turn_out("a1", [(hth, None)])
            hi(U_MOE - 1)
            act.wait_ge(wr_here, 16)
            nc.scalar.activation(wrs[:, :, 0:NE], wr[:], ACT.Copy).then_inc(wrh_done, 1)
            act.wait_ge(unit_used, U_MOE)
            hi(U_MOE, w=UNIT)
            sum_squares(3, False)
            hi(U_MOE + 1, w=UNIT)
            turn_out("n3", [(hth, G_FFN + DC)])
            for k in range(2, 4):
                hi(U_MOE + k, w=UNIT)
            act.wait_ge(v_done, 1)
            nc.scalar.activation(tops[:, 2, :], tops[:, 3, :], ACT.Exp).then_inc(e_done, 1)
            def gathered(v):
                for g in range(2):
                    act.wait_ge(m_gat, v * 2 + (g + 1))
                    for cc in range(4):
                        c = 4 * g + cc
                        last = nc.scalar.activation(hth[:, c, 0:P], ps[7 - g][:, cc * P:(cc + 1) * P], ACT.Copy,
                                                    scale=gcol[:, G_FFN + DC + c:G_FFN + DC + c + 1])
                    last.then_inc(m_hh, 1)

            gathered(0)

            act.wait_ge(tab_done, 1)
            runs = act.value_load(tab[0:1, 0:1], min_val=NE, max_val=NE + V_EXTRA)
            last_run = act.value_load(tab[0:1, 5:6], min_val=NE - 1, max_val=NE + V_EXTRA - 1)

            def y_out(v):
                act.wait_ge(unit_used, v * U_RUN + U_MOE)
                for n in range(2):
                    last = nc.scalar.activation(ye[:, n * 512:(n + 1) * 512], ps[4 + n][:, :], ACT.Copy)
                last.then_inc(m_ye, 1)

            def gt_hi(v, c):
                act.wait_ge(m_t, v * ESTEPS + (c + 1))
                nc.scalar.activation(gth[:], ps[6 + c % 2][:, :], ACT.Copy).then_inc(m_gh, 1)

            act.wait_ge(m_zero, 1)

            def run(v, final):
                def mhi(k):
                    if k < U_RUN or not final:
                        hi(U_MOE + k, v, U_RUN, UNIT)

                k = 0
                for c in range(ESTEPS):
                    mhi(k + 4)
                    if c:
                        mhi(k + 5)
                        gt_hi(v, c - 1)
                    else:
                        y_out(v)
                        mhi(k + 5)
                    act.wait_ge(unit_used, v * U_RUN + (U_MOE + k + 2))
                    nc.scalar.activation(ms[:, c % 2, :], ps[c % 2][:, :], ACT.Silu).then_inc(m_s, 1)
                    for i in range(2, 4 if c == 0 else 6):
                        mhi(k + 4 + i)
                    k += 4 if c == 0 else 6
                gt_hi(v, ESTEPS - 1)
                mhi(k + 4)
                mhi(k + 5)
                act.wait_ge(m_c, v + 1)
                nc.scalar.activation(cmb[:], ps[1][:, 0:SEQ], ACT.Copy).then_inc(m_cs, 1)
                if not final:
                    gathered(v + 1)

            with act.Fori(0, last_run) as v:
                run(v, False)
            run(last_run, True)
            y_out(runs)

        @block.vector
        def _(dve):
            steps = [0]

            def chain(ins):
                steps[0] += 1
                ins.then_inc(v_step, 1)
                dve.wait_ge(v_step, steps[0])


            def lo(n, j=0, j_units=0, w=None):
                moe_unit = n - U_MOE
                h, l = moe_slot(moe_unit) if moe_unit >= 0 else split_slot(n)
                w = width(n) if w is None else w
                dve.wait_ge(hi_done, n + 1 + j * j_units)
                nc.vector.tensor_tensor(l[:, 0:w], raw[:, n % RAW, 0:w], h[:, 0:w].bitcast(fp32),
                                        ALU.subtract).then_inc(lo_done, 1)

            def normalise(m):
                for t in range(T):
                    dve.wait_ge(rstd_done, T * m + t + 1)
                    nc.vector.tensor_scalar(tn[:, t, :], xr[:, t, :], rstd[:, t:t + 1], None, ALU.mult).then_inc(tn_done, 1)

            def turn_out(name, dsts):
                k = TURN[name]
                for b in range(TURN_BANKS):
                    dve.wait_ge(th_done, TURN_BANKS * k + b + 1)
                    for cc in range(2):
                        c = 2 * b + cc
                        src = ps[b][:, cc * SEQ:(cc + 1) * SEQ]
                        for h, l, g in dsts:
                            if g is None:
                                last = nc.vector.tensor_tensor(l[:, c, :], src, h[:, c, :].bitcast(fp32), ALU.subtract)
                            else:
                                last = nc.vector.scalar_tensor_tensor(l[:, c, :], src, gcol[:, g + c:g + c + 1],
                                                                      h[:, c, :].bitcast(fp32), ALU.mult, ALU.subtract)
                    last.then_inc(tl_done, 1)

            def add_residual(block, used, first_half=None):
                for n in range(2):
                    for t in range(T):
                        i = 2 * n + t
                        if i == 3:
                            dve.wait_ge(unit_used, used)
                        elif n == 0 and first_half is not None:
                            dve.wait_ge(unit_used, first_half)
                        else:
                            dve.wait_ge(y_done[block], i + 1 if first_half is None else 1)
                        piece = xr[:, t, n * 512:(n + 1) * 512]
                        nc.vector.tensor_tensor(piece, ps[4 + i][:, :], piece, ALU.add).then_inc(xr_done, 1)

            normalise(0)
            lo(0)
            dve.wait_ge(gcol_tr, 1)
            nc.vector.tensor_copy(gcol[:], ps[7][:, 0:G_ALL]).then_inc(gcol_done, 1)
            lo(1)
            dve.wait_ge(gcol_done, 1)
            turn_out("n0", [(hth, htl, G_ATT)])
            lo(2)
            lo(3)
            cq = tn[:, :, 0:Q_LORA]
            ckv = tn[:, :, Q_LORA:Q_LORA + KV_LORA]
            dve.wait_ge(rstd_lat, 1)
            for t in range(T):
                nc.vector.tensor_scalar(cq[:, t, :], ps[4 + t][:, 0:Q_LORA], rstd[:, t:t + 1], None, ALU.mult).then_inc(lat_tn, 1)
            lo(4)
            lo(5)
            dve.wait_ge(rstd_lat, 2)
            for t in range(T):
                nc.vector.tensor_copy(kpe[:, t, :], ps[6 + t][:, KV_LORA:KV_LORA + ROPE])
                nc.vector.tensor_scalar(ckv[:, t, :], ps[6 + t][:, 0:KV_LORA], rstd[:, T + t:T + t + 1], None, ALU.mult).then_inc(lat_tn, 1)
            for b in range(3):
                dve.wait_ge(lat_h, b + 1)
                for cc in range(2 if b < 2 else 1):
                    c = 2 * b + cc
                    last = nc.vector.scalar_tensor_tensor(cl[:, c, :], ps[b][:, cc * SEQ:(cc + 1) * SEQ],
                                                          gcol[:, G_CQ + c:G_CQ + c + 1], ch[:, c, :].bitcast(fp32),
                                                          ALU.mult, ALU.subtract)
                last.then_inc(lat_l, 1)
            for i in range(14):
                if i % 2 == 1:
                    dve.wait_ge(unit_used, latent_out(i)[0])
                    nc.vector.tensor_copy(latent_out(i)[1], ps[4 + i % 4][:, :]).then_inc(pj_v[0], 1)
                if i == 9:
                    dve.wait_ge(sq_done[0], 1)
                    dve.wait_ge(rope_tab, 2)
                    chain(rotate(nc.vector, 0))
                    nc.vector.tensor_tensor(q_rope(0), roptmp[:, 0, 0], roptmp[:, 0, 1], ALU.add).then_inc(rq_done, 1)
                if i in (1, 3, 5, 9):
                    lo({1: 6, 3: 7, 5: 8, 9: 9}[i])
                if i in (7, 11):
                    t = i // 4 - 1
                    dve.wait_ge(sq_done[0], t + 1)
                    nc.vector.reduce_sum(ssh[:, 0, t, :], squares[:, t * HEADS * QK:(t + 1) * HEADS * QK].rearrange("p (h w) -> p h w", w=QK),
                                         AX).then_inc(sh_done[0], 1)
            for i in range(2 * T):
                h, t = i // T, i % T
                at = (2 * t + h) * HEADS * NOPE // 2
                dve.wait_ge(sq_done[0], T + i + 1)
                nc.vector.reduce_sum(ssh[:, 1, t, h * HEADS // 2:(h + 1) * HEADS // 2],
                                     squares[:, at:at + HEADS * NOPE // 2].rearrange("p (h w) -> p h w", w=NOPE),
                                     AX).then_inc(sh_done[0], 1)
            dve.wait_ge(kps_done, 2)
            for t in range(T):
                dve.wait_ge(sh_done[0], 3 * T)
                last = nc.vector.tensor_scalar(ssh[:, 1, t, :], ssh[:, 1, t, :], ss[:, 4 + t:5 + t], None, ALU.add)
            chain(last)

            def head_roots(la, n):
                r, v = (a.rearrange("p a t h -> p (a t h)") for a in (rsh[:], ssh[:]))
                nc.vector.tensor_scalar(v, v, 1.0 / n, EPS, ALU.mult, ALU.add).then_inc(var_done[la], 1)
                dve.wait_ge(std_done[la], 1)
                chain(nc.vector.reciprocal(r, r))
                chain(nc.vector.tensor_tensor(rtmp[:], v, r, ALU.mult))
                chain(nc.vector.tensor_tensor(rtmp[:], rtmp[:], r, ALU.mult))
                chain(nc.vector.tensor_scalar(rtmp[:], rtmp[:], -0.5, 1.5, ALU.mult, ALU.add))
                nc.vector.tensor_tensor(r, r, rtmp[:], ALU.mult).then_inc(rs_done[la], 1)

            head_roots(0, QK)
            def attention(la):
                a = A[la]
                hw = QK if la == 0 else HD

                def scale_q(p, par, first=False):
                    if not first:
                        dve.wait_ge(a["tq"], p - 1)
                    dst = qn[:, par, :, 0:2 * hw].rearrange("p t (h w) -> p t h w", h=2)
                    src = (q_all[:] if la == 0 else q1).rearrange("p t (h w) -> p t h w", h=HEADS)[:, :, ds(p * 2, 2), :]
                    nc.vector.tensor_tensor(dst, src, rsh[:, 0, :, ds(p * 2, 2)].unsqueeze(3).to_broadcast([P, T, 2, hw]),
                                            ALU.mult).then_inc(a["qn"], 1)

                def k_out(p, par):
                    dve.wait_ge(a["tk"], p + 1)
                    for rows_, cols in (((0, QK), (0, 2 * SEQ)),) if la == 0 else (((0, HD), (0, SEQ)), ((HD, P), (SEQ, 2 * SEQ))):
                        rs, src = slice(*rows_), slice(0, cols[1] - cols[0])
                        last = nc.vector.tensor_scalar(kT[rs, par, cols[0]:cols[1]], ps[1][rs, src], qkg[rs, la, 1:2], None, ALU.mult)
                    last.then_inc(a["kT"], 1)

                def maxima(p, par, h):
                    dve.wait_ge(a["s"], p * 2 + (h + 1))
                    src = ps[2 + h]
                    if la == 1:
                        if h == 0:
                            dve.wait_ge(bias_here[par], (p - par) * 8 + 16)
                        src = bias[:, par, h, :]
                        nc.vector.tensor_tensor(src, ps[2 + h][:, 0:SPAN], src, ALU.add).then_inc(a["sb"], 1)
                        dve.wait_ge(a["sb"], p * 2 + (h + 1))
                    for t, (lo_, n_) in enumerate(((0, P), (P, SEQ))):
                        last = nc.vector.tensor_reduce(nmax[:, par, t, h:h + 1], src[:, lo_:lo_ + n_], axis=AX,
                                                       op=ALU.max, negate=True)
                    last.then_inc(a["nm"], 1)

                def pt_out(p, par):
                    dve.wait_ge(a["pt"], p * 2 + 2)
                    nc.vector.tensor_copy(probT[:, par, 1, :], ps[5][:, 0:SPAN]).then_inc(a["pv"], 1)

                def out_(p, par):
                    dve.wait_ge(a["ex"], p * 2 + 2)
                    nc.vector.reciprocal(rinv[:, par], rsum[:, par]).then_inc(a["ri"], 1)
                    dve.wait_ge(a["ri"], p + 1)
                    dve.wait_ge(a["o"], p + 1)
                    nc.vector.tensor_tensor(tn[:].rearrange("p t (h w) -> p t h w", h=HEADS)[:, :, ds(p * 2, 2), :],
                                            ps[6 + par][:, 0:T * 2 * VDIM].rearrange("p (t h w) -> p t h w", t=T, h=2),
                                            rinv[:, par].unsqueeze(3).to_broadcast([P, T, 2, VDIM]),
                                            ALU.mult).then_inc(a["oo"], 1)

                def step(p, par, first=False, more=True):
                    maxima(p, par, 1)
                    k_out(p + 1, 1 - par)
                    if not first:
                        out_(p - 1, 1 - par)
                    if more:
                        scale_q(p + 2, par)
                    maxima(p + 1, 1 - par, 0)
                    pt_out(p, par)

                scale_q(0, 0, first=True)
                scale_q(1, 1, first=True)
                yield
                if la == 1:
                    dve.wait_ge(zeroed, 2)
                k_out(0, 0)
                yield
                maxima(0, 0, 0)
                step(0, 0, first=True)
                step(1, 1)
                with dve.Fori(1, PAIRS // 2 - 1) as j:
                    for u in range(2):
                        step(j * 2 + u, u)
                step(PAIRS - 2, 0, more=False)
                maxima(PAIRS - 1, 1, 1)
                out_(PAIRS - 2, 0)
                pt_out(PAIRS - 1, 1)
                out_(PAIRS - 1, 1)
                yield

            dve.wait_ge(rs_done[0], 1)
            dve.wait_ge(rq_done, 2)
            dve.wait_ge(rope_tab, 2)
            for _ in attention(0):
                pass
            turn_out("a0", [(hth, htl, None)])
            for n in range(U_WO0 + 1, U_FFN + 2):
                lo(n)
            add_residual(0, U_WO0 + 4, U_WO0 + 2)
            normalise(1)
            lo(U_FFN + 2)
            turn_out("n1", [(hth, htl, G_FFN)])

            def f_gate(c, par):
                dve.wait_ge(unit_used, U_FFN + 2 if isinstance(c, int) else c * 3 + (U_FFN + 1))
                dve.wait_ge(f_s, c + 1)
                nc.vector.tensor_tensor(fg[:, par, :], ps[2 + par][:, :], fs[:, par, :], ALU.mult).then_inc(f_g, 1)

            def f_lo(c, par):
                dve.wait_ge(f_gh, c + 1)
                nc.vector.tensor_tensor(fgl[:, par, :], fg[:, par, :], fgh[:, par, :].bitcast(fp32), ALU.subtract).then_inc(f_gl, 1)

            f_gate(0, 0)
            lo(U_FFN + 3)
            f_lo(0, 0)
            with dve.Fori(0, (FSTEPS - 1) // 2) as j:
                for u in range(2):
                    n = U_FFN + 4 + 3 * u
                    lo(n, j, 6)
                    lo(n + 1, j, 6)
                    f_gate(j * 2 + (u + 1), 1 - u)
                    lo(n + 2, j, 6)
                    f_lo(j * 2 + (u + 1), 1 - u)
            lo(U_L1 + 1)
            add_residual(1, U_L1)
            normalise(2)
            turn_out("n2", [(hth, htl, G_ATT + DC)])
            for c in range(DC):
                if c % 2 == 0:
                    dve.wait_ge(h2_hi, c // 2 + 1)
                last = nc.vector.scalar_tensor_tensor(h2l[:, c, :], ps[c // 2][:, c % 2 * SEQ:(c % 2 + 1) * SEQ],
                                                      gcol[:, G_KV + c:G_KV + c + 1], h2h[:, c, :].bitcast(fp32),
                                                      ALU.mult, ALU.subtract)
                if c % 2:
                    last.then_inc(h2_done, 1)
            for g in range(6):
                if g == 5:
                    att1 = attention(1)
                    next(att1)
                lo(U_L1 + 2 + 2 * g)
                lo(U_L1 + 3 + 2 * g)
                if g == 5:
                    next(att1)
                dve.wait_ge(unit_used, U_L1 + 2 + 2 * g)
                nc.vector.tensor_copy((q1, k1, v1)[g // 2][:, 1, (g % 2) * 512:(g % 2 + 1) * 512],
                                      ps[5 + g % 2 * 2][:, :]).then_inc(pj_v[1], 1)
                if g in (1, 3):
                    for t in range(T):
                        dve.wait_ge(sq_done[1], g - 1 + t + 1)
                        nc.vector.reduce_sum(ssh[:, g // 2, t, :], squares1[:, t * D:(t + 1) * D].rearrange("p (h w) -> p h w", w=HD),
                                             AX).then_inc(sh_done[1], 1)
                if g == 3:
                    dve.wait_ge(sh_done[1], 4)
                    head_roots(1, HD)
                    dve.wait_ge(rs_done[1], 1)
            next(att1)
            turn_out("a1", [(hth, htl, None)])
            lo(U_MOE - 2)
            lo(U_MOE - 1)
            dve.wait_ge(wrh_done, 1)
            nc.vector.tensor_tensor(wrs[:, :, NE:2 * NE], wr[:], wrs[:, :, 0:NE].bitcast(fp32), ALU.subtract).then_inc(wrl_done, 1)
            add_residual(2, U_MOE, U_MOE - 2)
            lo(U_MOE, w=UNIT)
            normalise(3)
            lo(U_MOE + 1, w=UNIT)
            turn_out("n3", [(hth, htl, G_FFN + DC)])

            def bc(a):
                return a.unsqueeze(2).to_broadcast([P, T, NE])

            def gathered(v):
                for g in range(2):
                    dve.wait_ge(m_hh, v * 2 + (g + 1))
                    for cc in range(4):
                        c = 4 * g + cc
                        last = nc.vector.scalar_tensor_tensor(htl[:, c, 0:P], ps[7 - g][:, cc * P:(cc + 1) * P],
                                                      gcol[:, G_FFN + DC + c:G_FFN + DC + c + 1],
                                                      hth[:, c, 0:P].bitcast(fp32), ALU.mult, ALU.subtract)
                    last.then_inc(m_hl, 1)

            V = nc.vector
            sel1, sel2, sel, gate, tmp, posm = (work[:, i] for i in range(6))
            v1_, v2_, e2, dv, g1_, g2_ = (tops[:, i] for i in range(6))
            dve.wait_ge(lg_mm, 1)
            V.tensor_copy(lgt[:], ps[4][0:2 * NE, 0:SEQ]).then_inc(lg_out, 1)
            dve.wait_ge(lg_tr, 1)
            parts = ps[5][:, 0:T * 2 * NE].rearrange("p (t s e) -> p t s e", t=T, s=2)
            chain(V.tensor_copy(lg[:], parts[:, :, 0, :]))
            chain(V.tensor_tensor(lg[:], parts[:, :, 1, :], lg[:], ALU.add))

            def first_max(src, val, one_hot):
                chain(V.tensor_reduce(val, src, axis=AX, op=ALU.max))
                chain(V.tensor_tensor(tmp, src, bc(val), ALU.is_equal))
                chain(V.tensor_tensor(tmp, tmp, rev, ALU.mult))
                chain(V.tensor_reduce(g1_, tmp, axis=AX, op=ALU.max))
                chain(V.tensor_tensor(one_hot, tmp, bc(g1_), ALU.is_equal))

            first_max(lg[:], v1_, sel1)
            chain(V.scalar_tensor_tensor(posm, sel1, -3e38, lg[:], ALU.mult, ALU.add))
            first_max(posm, v2_, sel2)
            V.tensor_tensor(sel, sel1, sel2, ALU.add).then_inc(sel_done, 1)
            V.tensor_tensor(dv, v2_, v1_, ALU.subtract).then_inc(v_done, 1)
            lo(U_MOE + 2, w=UNIT)
            dve.wait_ge(pos_mm, 1)
            pp = ps[5][:, 0:T * NE].rearrange("p (t e) -> p t e", t=T)
            cnt = ps[5][:, T * NE:(T + 1) * NE]
            chain(V.scalar_tensor_tensor(posm, pp, 1.0, sel, ALU.add, ALU.mult))
            chain(V.tensor_scalar(posm, posm, -1.0, None, ALU.add))
            for t in range(T):
                V.tensor_scalar(pick[:, t, :], iota, posm[:, t, 0:1], None, ALU.is_equal).then_inc(m_pick, 1)
            big, rank, shift = over[:, 0], over[:, 1], work[:, 6]
            V.tensor_scalar(shift, posm, -float(P), None, ALU.add)
            chain(V.tensor_scalar(big, cnt, float(P), None, ALU.is_gt))
            V.reduce_sum(tabf[:, 1:2], big, AX)
            chain(V.tensor_tensor(prior[:], before, big.unsqueeze(1).to_broadcast([P, NE, NE]), ALU.mult))
            chain(V.reduce_sum(rank, prior[:], AX))
            V.tensor_scalar(tabf[:, 0:1], tabf[:, 1:2], float(NE), None, ALU.add)
            V.tensor_scalar(tabf[:, 5:6], tabf[:, 1:2], float(NE - 1), None, ALU.add)
            chain(V.tensor_tensor(hot[:], nth, rank.unsqueeze(1).to_broadcast([P, V_EXTRA, NE]), ALU.is_equal))
            chain(V.tensor_tensor(hot[:], hot[:], big.unsqueeze(1).to_broadcast([P, V_EXTRA, NE]), ALU.mult))
            chain(V.tensor_tensor(prior[:, 0:V_EXTRA, :], hot[:], number, ALU.mult))
            chain(V.reduce_sum(tabf[:, 2:2 + V_EXTRA], prior[:, 0:V_EXTRA, :], AX))
            V.memset(cmb[:], 0.0).then_inc(m_cs, 1)
            V.tensor_copy(tab[:, 0:6], tabf[:, 0:6]).then_inc(tab_done, 1)
            hot_b = hot[:].unsqueeze(2).to_broadcast([P, V_EXTRA, T, NE])
            V.memset(pos_v[:, NE:, :], -1.0)
            V.memset(gate_v[:, NE:, :], 0.0)
            chain(V.tensor_tensor(hot_t[:], hot_b, shift.unsqueeze(1).to_broadcast([P, V_EXTRA, T, NE]), ALU.mult))
            V.tensor_copy(pos_v[:, 0:NE, :].rearrange("p e t -> p t e"), posm)
            chain(V.tensor_reduce(pos_v[:, NE:NE + V_EXTRA, :], hot_t[:], axis=AX, op=ALU.add))
            lo(U_MOE + 3, w=UNIT)
            gathered(0)
            dve.wait_ge(e_done, 1)
            chain(V.tensor_scalar(g1_, e2, 1.0, None, ALU.add))
            chain(V.reciprocal(g1_, g1_))
            chain(V.tensor_tensor(g2_, e2, g1_, ALU.mult))
            V.tensor_tensor(tmp, sel2, bc(g2_), ALU.mult)
            chain(V.tensor_tensor(gate, sel1, bc(g1_), ALU.mult))
            chain(V.tensor_tensor(gate, gate, tmp, ALU.add))
            V.tensor_copy(gate_v[:, 0:NE, :].rearrange("p e t -> p t e"), gate)
            chain(V.tensor_tensor(hot_t[:], hot_b, gate.unsqueeze(1).to_broadcast([P, V_EXTRA, T, NE]), ALU.mult))
            chain(V.tensor_reduce(gate_v[:, NE:NE + V_EXTRA, :], hot_t[:], axis=AX, op=ALU.add))
            dve.wait_ge(tab_done, 1)
            runs = dve.value_load(tab[0:1, 0:1], min_val=NE, max_val=NE + V_EXTRA)
            last_run = dve.value_load(tab[0:1, 5:6], min_val=NE - 1, max_val=NE + V_EXTRA - 1)

            def gt_lo(v, c):
                dve.wait_ge(m_gh, v * ESTEPS + (c + 1))
                V.tensor_tensor(gtl[:], ps[6 + c % 2][:, :], gth[:].bitcast(fp32), ALU.subtract).then_inc(m_gl, 1)

            def add_run(v):
                for n in range(2):
                    for t in range(T):
                        i = 2 * n + t
                        dve.wait_ge(m_cmb, v * 4 + (i + 1))
                        piece = xr[:, t, n * 512:(n + 1) * 512]
                        V.tensor_tensor(piece, ps[6 + i % 2][:, :], piece, ALU.add).then_inc(m_add, 1)

            def one_hots(v):
                dve.wait_ge(m_gat, v * 2 + 2)
                dve.wait_ge(m_pick, v * 4 + 2)
                V.tensor_copy(cur[:, 0:1, :], pos_v[:, ds(v + 1, 1), :]).then_inc(m_cur, 1)
                V.tensor_copy(cur[:, 1:2, :], pos_v[:, ds(v, 1), :]).then_inc(m_cur, 1)
                V.tensor_copy(cur[:, 2:3, :], gate_v[:, ds(v, 1), :]).then_inc(m_cur, 1)
                dve.wait_ge(m_cur, v * 3 + 3)
                for t in range(T):
                    V.tensor_scalar(gpick[:, t, :], iota, cur[:, 1, t:t + 1], cur[:, 2, t:t + 1],
                                    ALU.is_equal, ALU.mult).then_inc(m_pick, 1)
                for t in range(T):
                    V.tensor_scalar(pick[:, t, :], iota, cur[:, 0, t:t + 1], None, ALU.is_equal).then_inc(m_pick, 1)

            def run(v, final):
                def mlo(k):
                    if k < U_RUN or not final:
                        lo(U_MOE + k, v, U_RUN, UNIT)

                k = 0
                for c in range(ESTEPS):
                    mlo(k + 4)
                    mlo(k + 5)
                    if c:
                        gt_lo(v, c - 1)
                    else:
                        add_run(v)
                    for i in range(2, 4):
                        mlo(k + 4 + i)
                    if c == 1:
                        one_hots(v)
                    dve.wait_ge(unit_used, v * U_RUN + (U_MOE + k + 4))
                    dve.wait_ge(m_s, v * ESTEPS + (c + 1))
                    V.tensor_tensor(mg[:], ps[2 + c % 2][:, :], ms[:, c % 2, :], ALU.mult).then_inc(m_g, 1)
                    for i in range(4, 4 if c == 0 else 6):
                        mlo(k + 4 + i)
                    k += 4 if c == 0 else 6
                gt_lo(v, ESTEPS - 1)
                mlo(k + 4)
                mlo(k + 5)
                if not final:
                    gathered(v + 1)

            with dve.Fori(0, last_run) as v:
                run(v, False)
            run(last_run, True)
            add_run(runs)

        @block.tensor
        def _(pe):
            mm = nc.tensor.matmul

            def tr(dst, src, np_=P):
                return nc.tensor.transpose(dst, src, ident[0:np_, 0:np_])

            def mm3(dst, xh, xl, wh, wl, start, stop, flip=False):
                for i, (a, b) in enumerate(((xh, wh), (xl, wh), (xh, wl)) if flip else ((xh, wh), (xh, wl), (xl, wh))):
                    last = mm(dst, b if flip else a, a if flip else b, start=start and i == 0, stop=stop and i == 2)
                return last

            def turn(name, waits):
                for t in range(T):
                    pe.wait_ge(*waits[t])
                    for b in range(TURN_BANKS):
                        for cc in range(2):
                            c = 2 * b + cc
                            last = tr(ps[b][:, cc * SEQ + t * P:cc * SEQ + (t + 1) * P], tn[:, t, c * P:(c + 1) * P])
                        if t == T - 1:
                            last.then_inc(tr_done, 1)

            def turned(name, c=DC - 1, first=True):
                if first:
                    pe.wait_ge(tl_done, TURN_BANKS * TURN[name] + c // 2 + 1)

            def ready(n, j=0, j_units=0):
                pe.wait_ge(lo_done, n + 1 + j * j_units)

            pe.wait_ge(c_here, 16)
            turn("n0", [(tn_done, 1), (tn_done, 2)])
            pe.wait_ge(g_here, 16 * 5)
            tr(ps[7][:, 0:G_ALL], grow[:], G_ALL).then_inc(gcol_tr, 1)

            for u, bank, w in ((U_DQ, 4, Q_LORA), (U_DKV, 6, KV_LORA + ROPE)):
                for h in range(2):
                    ready(u + h)
                    wh, wl = split_slot(u + h)
                    for t in range(T):
                        for cc in range(4):
                            c = 4 * h + cc
                            turned("n0", c, u == U_DQ and t == 0 and c % 2 == 0)
                            last = mm3(ps[bank + t][:, 0:w], hth[:, c, t * P:(t + 1) * P], htl[:, c, t * P:(t + 1) * P],
                                       wh[:, cc * w:(cc + 1) * w], wl[:, cc * w:(cc + 1) * w], c == 0, c == DC - 1)
                    last.then_inc(unit_used, 1)
            for b in range(3):
                pe.wait_ge(lat_tn, 2 if b == 0 else 4)
                for cc in range(2 if b < 2 else 1):
                    c = 2 * b + cc
                    for t in range(T):
                        last = tr(ps[b][:, cc * SEQ + t * P:cc * SEQ + (t + 1) * P], tn[:, t, c * P:(c + 1) * P])
                last.then_inc(lat_tr, 1)
            pe.wait_ge(lat_l, 3)

            def free_bank(i, la):
                if i >= 4:
                    pe.wait_ge((pj_a if i % 2 == 0 else pj_v)[la], (i - 4) // 2 + 1)

            i = 0
            for n in range(3):
                ready(U_UQ + n)
                wh, wl = split_slot(U_UQ + n)
                for t in range(T):
                    free_bank(i, 0)
                    for c in range(QC):
                        last = mm3(ps[4 + i % 4][:, :], ch[:, c, t * P:(t + 1) * P], cl[:, c, t * P:(t + 1) * P],
                                   wh[:, c * 512:(c + 1) * 512], wl[:, c * 512:(c + 1) * 512], c == 0, c == QC - 1)
                    i += 1
                last.then_inc(unit_used, 1)
            for n in range(2):
                ready(U_UKV + n)
                wh, wl = split_slot(U_UKV + n)
                for s in range(2):
                    for t in range(T):
                        free_bank(i, 0)
                        for c in range(KVC):
                            at = c * 1024 + s * 512
                            last = mm3(ps[4 + i % 4][:, :], ch[:, QC + c, t * P:(t + 1) * P], cl[:, QC + c, t * P:(t + 1) * P],
                                       wh[:, at:at + 512], wl[:, at:at + 512], c == 0, c == KVC - 1)
                        i += 1
                last.then_inc(unit_used, 1)

            def attention(la):
                a = A[la]
                hw = QK if la == 0 else HD
                v_src = kv_all[:].rearrange("p t (h w) -> p t h w", h=HEADS) if la == 0 else v1.rearrange("p t (h w) -> p t h w", h=HEADS)
                v_at = NOPE if la == 0 else 0

                def turn_pair(p, par, first=False):
                    for src, bank, made, out_, done in ((qn, 0, "qn", "qT", "tq"), (kn, 1, "kn", "kT", "tk")):
                        pe.wait_ge(a[made], p + 1)
                        if not first:
                            pe.wait_ge(a[out_], p)
                        if la == 0:
                            for h in range(2):
                                for t in range(T):
                                    last = tr(ps[bank][0:QK, h * SEQ + t * P:h * SEQ + (t + 1) * P],
                                              src[:, par, t, h * QK:(h + 1) * QK])
                        else:
                            for t in range(T):
                                last = tr(ps[bank][:, t * P:(t + 1) * P], src[:, par, t, 0:2 * HD])
                        last.then_inc(a[done], 1)

                def scores(p, par, h, first=False):
                    if h == 0:
                        pe.wait_ge(a["qT"], p + 1)
                        pe.wait_ge(a["kT"], p + 1)
                    if not first:
                        pe.wait_ge(a["ex" if la == 0 else "sb"], p * 2 + (h - 1))
                    part = slice(0, QK if la == 0 else P)
                    q_at = h * SEQ if la == 0 else 0
                    for t, (lo_, keys) in enumerate(((0, P), (P, SEQ))):
                        mm(ps[2 + h][:, lo_:lo_ + keys], qT[part, par, q_at + t * P:q_at + (t + 1) * P],
                           kT[part, par, h * SEQ:h * SEQ + keys], start=True, stop=False)
                        last = mm(ps[2 + h][:, lo_ + keys - CHUNK:lo_ + keys], mask_row, mask_col, start=False, stop=True)
                    last.then_inc(a["s"], 1)

                def turn_probs(p, par, h, first=False):
                    pe.wait_ge(a["ex"], p * 2 + (h + 1))
                    if not first:
                        pe.wait_ge(a["pa" if h == 0 else "pv"], p)
                    for b in range(3):
                        last = tr(ps[4 + h][:, b * P:(b + 1) * P], prob[:, par, h, b * P:(b + 1) * P])
                    last.then_inc(a["pt"], 1)

                def values(p, par, h, first=False):
                    pe.wait_ge(a["pa" if h == 0 else "pv"], p + 1)
                    if h == 0 and not first:
                        pe.wait_ge(a["oo"], p - 1)
                    for t in range(T):
                        dst = ps[6 + par][:, (2 * t + h) * VDIM:(2 * t + h + 1) * VDIM]
                        for kt in range(t + 1):
                            last = mm(dst, probT[:, par, h, (t + kt) * P:(t + kt + 1) * P],
                                      v_src[:, kt:kt + 1, ds(p * 2 + h, 1), v_at:v_at + VDIM],
                                      start=kt == 0, stop=kt == t)
                    if h == 1:
                        last.then_inc(a["o"], 1)

                turn_pair(0, 0, first=True)
                yield
                pe.wait_ge(mask_done, 1)
                scores(0, 0, 0, first=True)

                def step(p, par, first=False, second=False):
                    scores(p, par, 1, first=first)
                    turn_pair(p + 1, 1 - par)
                    turn_probs(p, par, 0, first=first)
                    if not first:
                        values(p - 1, 1 - par, 1)
                    scores(p + 1, 1 - par, 0)
                    turn_probs(p, par, 1, first=first)
                    values(p, par, 0, first=first or second)

                step(0, 0, first=True)
                step(1, 1, second=True)
                with pe.Fori(1, PAIRS // 2 - 1) as j:
                    for u in range(2):
                        step(j * 2 + u, u)
                step(PAIRS - 2, 0)
                scores(PAIRS - 1, 1, 1)
                turn_probs(PAIRS - 1, 1, 0)
                values(PAIRS - 2, 0, 1)
                turn_probs(PAIRS - 1, 1, 1)
                values(PAIRS - 1, 1, 0)
                values(PAIRS - 1, 1, 1)
                yield

            def out_proj(la, u0):
                for n in range(2):
                    for h in range(2):
                        ready(u0 + 2 * n + h)
                        wh, wl = split_slot(u0 + 2 * n + h)
                        for t in range(T):
                            for cc in range(4):
                                c = 4 * h + cc
                                turned(f"a{la}", c, n == 0 and t == 0 and c % 2 == 0)
                                last = mm3(ps[4 + 2 * n + t][:, :], hth[:, c, t * P:(t + 1) * P], htl[:, c, t * P:(t + 1) * P],
                                           wh[:, cc * 512:(cc + 1) * 512], wl[:, cc * 512:(cc + 1) * 512], c == 0, c == DC - 1)
                            if n == 1 and h == 1 and t == 0:
                                last.then_inc(y_done[2 * la], 1)
                        last.then_inc(unit_used, 1)

            for _ in attention(0):
                pass
            turn("a0", 2 * [(A[0]["oo"], PAIRS)])
            out_proj(0, U_WO0)

            turn("n1", [(tn_done, 3), (tn_done, 4)])

            def up(c, par, n, j=0, j_units=0, first=False):
                for w, bank in enumerate((0, 2)):
                    ready(n + w, j, j_units)
                    wh, wl = split_slot(n + w)
                    for f in range(2):
                        for cc in range(DC):
                            at = cc * FW + f * P
                            turned("n1", cc, first and w == 0 and f == 0 and cc % 2 == 0)
                            last = mm3(ps[bank + par][:, f * SEQ:(f + 1) * SEQ], hth[:, cc, :], htl[:, cc, :],
                                       wh[:, at:at + P], wl[:, at:at + P], cc == 0, cc == DC - 1, flip=True)
                    last.then_inc(unit_used, 1)

            def down(c, par, n, first, last_, j=0, j_units=0):
                ready(n, j, j_units)
                pe.wait_ge(f_gl, c + 1)
                wh, wl = split_slot(n)
                for half in range(2):
                    for t in range(T):
                        for f in range(2):
                            g = slice(f * SEQ + t * P, f * SEQ + (t + 1) * P)
                            at = f * D + half * 512
                            last = mm3(ps[4 + 2 * half + t][:, :], fgh[:, par, g], fgl[:, par, g],
                                       wh[:, at:at + 512], wl[:, at:at + 512], first and f == 0, last_ and f == 1)
                        if last_ and (half, t) != (1, T - 1):
                            last.then_inc(y_done[1], 1)
                last.then_inc(unit_used, 1)

            def ffn_step(c, par, n, first=False, j=0, j_units=0):
                up(c + 1, 1 - par, n, j, j_units)
                down(c, par, n + 2, first, False, j, j_units)

            up(0, 0, U_FFN, first=True)
            ffn_step(0, 0, U_FFN + 2, first=True)
            ffn_step(1, 1, U_FFN + 5)
            with pe.Fori(1, (FSTEPS - 1) // 2) as j:
                for u in range(2):
                    ffn_step(j * 2 + u, u, U_FFN + 2 + 3 * u, j=j, j_units=6)
            down(FSTEPS - 1, 0, U_L1 - 1, False, True)

            turn("n2", [(tn_done, 5), (tn_done, 6)])
            i = 0
            for w in range(3):
                xh, xl = (hth, htl) if w == 0 else (h2h, h2l)
                for n in range(2):
                    for h in range(2):
                        u = U_L1 + 4 * w + 2 * n + h
                        if u == U_MOE - 5:
                            att1 = attention(1)
                            next(att1)
                        ready(u)
                        wh, wl = split_slot(u)
                        for t in range(T):
                            if h == 0:
                                free_bank(i + t, 1)
                            for cc in range(4):
                                c = 4 * h + cc
                                turned("n2", c, w == 0 and n == 0 and t == 0 and c % 2 == 0)
                                if w == 1 and n == 0 and t == 0 and c % 2 == 0:
                                    pe.wait_ge(h2_done, c // 2 + 1)
                                last = mm3(ps[4 + (i + t) % 4][:, :], xh[:, c, t * P:(t + 1) * P], xl[:, c, t * P:(t + 1) * P],
                                           wh[:, cc * 512:(cc + 1) * 512], wl[:, cc * 512:(cc + 1) * 512], c == 0, c == DC - 1)
                        last.then_inc(unit_used, 1)
                    i += 2
            for _ in att1:
                pass
            turn("a1", 2 * [(A[1]["oo"], PAIRS)])
            out_proj(1, U_MOE - 4)

            turn("n3", [(tn_done, 7), (tn_done, 8)])
            pe.wait_ge(wrl_done, 1)
            for c in range(DC):
                turned("n3", c, c % 2 == 0)
                for i, x_ in enumerate((hth, htl)):
                    last = mm(ps[4][0:2 * NE, 0:SEQ], wrs[:, c, :], x_[:, c, :], start=c == 0 and i == 0,
                              stop=c == DC - 1 and i == 1)
            last.then_inc(lg_mm, 1)
            pe.wait_ge(lg_out, 1)
            for t in range(T):
                last = tr(ps[5][:, t * 2 * NE:(t + 1) * 2 * NE], lgt[:, t * P:(t + 1) * P], 2 * NE)
            last.then_inc(lg_tr, 1)
            pe.wait_ge(sel_done, 1)
            sel = work[:, 2]
            mm(ps[5][:, 0:NE], tri, sel[:, 0, :], start=True, stop=True)
            for dst, m in ((1, tri), (2, ones)):
                mm(ps[5][:, dst * NE:(dst + 1) * NE], ones, sel[:, 0, :], start=True, stop=False)
                last = mm(ps[5][:, dst * NE:(dst + 1) * NE], m, sel[:, 1, :], start=False, stop=True)
            last.then_inc(pos_mm, 1)

            def gather():
                for g in range(2):
                    for cc in range(4):
                        c = 4 * g + cc
                        for t in range(T):
                            last = mm(ps[7 - g][:, cc * P:(cc + 1) * P], tn[:, t, c * P:(c + 1) * P], pick[:, t, :],
                                      start=t == 0, stop=t == T - 1)
                    last.then_inc(m_gat, 1)
                    yield

            pe.wait_ge(m_pick, 2)
            for _ in gather():
                pass

            pe.wait_ge(tab_done, 1)
            runs = pe.value_load(tab[0:1, 0:1], min_val=NE, max_val=NE + V_EXTRA)
            last_run = pe.value_load(tab[0:1, 5:6], min_val=NE - 1, max_val=NE + V_EXTRA - 1)
            pe.wait_ge(m_cs, 1)
            for n in range(2):
                last = mm(ps[4 + n][:, :], cmb[:, 0:P], tn[:, 0, n * 512:(n + 1) * 512], start=True, stop=True)
            last.then_inc(m_zero, 1)

            def combine(v):
                pe.wait_ge(m_ye, v + 1)
                pe.wait_ge(m_cs, v + 1)
                for i in range(4):
                    n, t = i // 2, i % 2
                    if i >= 2:
                        pe.wait_ge(m_add, v * 4 + (i - 1))
                    mm(ps[6 + i % 2][:, :], cmb[:, t * P:(t + 1) * P], ye[:, n * 512:(n + 1) * 512],
                       start=True, stop=True).then_inc(m_cmb, 1)

            def run(v, final):
                def eup(k, bank, c, h):
                    ready(U_MOE + k, v, U_RUN)
                    wh, wl = moe_slot(k)
                    for cc in range(4):
                        cd = 4 * h + cc
                        last = mm3(ps[bank + c % 2][:, :], hth[:, cd, 0:P], htl[:, cd, 0:P],
                                   wh[:, cc * EW:(cc + 1) * EW], wl[:, cc * EW:(cc + 1) * EW], cd == 0, cd == DC - 1)
                    last.then_inc(unit_used, 1)

                def edown(k, c):
                    pe.wait_ge(m_gl, v * ESTEPS + (c + 1))
                    for n in range(2):
                        ready(U_MOE + k + n, v, U_RUN)
                        wh, wl = moe_slot(k + n)
                        for f in range(4):
                            last = mm3(ps[4 + n][:, :], gth[:, f * P:(f + 1) * P], gtl[:, f * P:(f + 1) * P],
                                       wh[:, f * 512:(f + 1) * 512], wl[:, f * 512:(f + 1) * 512],
                                       c == 0 and f == 0, c == ESTEPS - 1 and f == 3)
                        last.then_inc(unit_used, 1)

                def eturn(c):
                    pe.wait_ge(m_g, v * ESTEPS + (c + 1))
                    for f in range(4):
                        last = tr(ps[6 + c % 2][:, f * P:(f + 1) * P], mg[:, f * P:(f + 1) * P])
                    last.then_inc(m_t, 1)

                pe.wait_ge(m_hl, v * 2 + 2)
                k = 0
                for c in range(ESTEPS):
                    eup(k, 0, c, 0)
                    eup(k + 1, 0, c, 1)
                    if c == 0:
                        combine(v)
                    else:
                        if c == 1:
                            pe.wait_ge(m_add, v * 4 + 4)
                        eturn(c - 1)
                    eup(k + 2, 2, c, 0)
                    eup(k + 3, 2, c, 1)
                    k += 4
                    if c:
                        edown(k, c - 1)
                        k += 2
                eturn(ESTEPS - 1)
                pe.wait_ge(m_pick, v * 4 + 6)
                for t in range(T):
                    last = tr(ps[1][:, t * P:(t + 1) * P], gpick[:, t, :])
                last.then_inc(m_c, 1)
                if not final:
                    halves = gather()
                    next(halves)
                    pe.wait_ge(m_gl, v * ESTEPS + ESTEPS)
                    next(halves)
                edown(k, ESTEPS - 1)

            with pe.Fori(0, last_run) as v:
                run(v, False)
            run(last_run, True)
            combine(runs)


_ORDER = ["x", "attn_norm", "ffn_norm", "a_w_dq", "a_g_cq", "a_w_uq", "a_w_dkv", "a_g_ckv", "a_w_ukv", "a_g_qn",
          "a_g_kn", "a_w_o", "kv_norm", "kv_w_k", "kv_w_v", "kv_g_kn", "b_w_q", "b_g_qn", "b_rel_bias", "b_w_o",
          "ffn_w1", "ffn_w3", "ffn_w2", "moe_router", "moe_w1", "moe_w3", "moe_w2"]


def _constants():
    import numpy as np

    c = np.zeros((P, C_ALL), np.float32)
    c[:, C_ID:C_ID + P] = np.eye(P)
    c[:, C_TRI:C_TRI + P] = np.triu(np.ones((P, P)), 1)
    c[:, C_IOTA:C_IOTA + P] = np.arange(P)
    c[:, C_ONES:C_ONES + P] = 1
    inv = np.float32(10000.0) ** (-np.arange(HALF, dtype=np.float32) / np.float32(HALF))
    angle = (np.arange(SEQ, dtype=np.float32)[:, None] * inv[None, :]).astype(np.float32)
    cos, sin = (f(angle.astype(np.float64)).reshape(T, P, HALF).transpose(1, 0, 2) for f in (np.cos, np.sin))
    c[:, C_ROPC:C_ROPC + T * ROPE] = np.concatenate([cos, cos], -1).reshape(P, -1)
    c[:, C_ROPS:C_ROPS + T * ROPE] = np.concatenate([-sin, sin], -1).reshape(P, -1)
    c[:, C_REV:C_REV + T * NE] = np.tile(NE - np.arange(NE), T)
    c[:, C_BEF:C_BEF + NE * NE] = np.tril(np.ones((NE, NE)), -1).reshape(-1)
    c[:, C_I3:C_I3 + V_EXTRA * NE] = np.repeat(np.arange(V_EXTRA), NE)
    c[:, C_E3:C_E3 + V_EXTRA * NE] = np.tile(np.arange(NE), V_EXTRA)
    c[0, C_MA:C_MA + CHUNK] = 1
    c[0, C_MB:C_MB + CHUNK] = MASKED
    return c


def kernel(**inputs):
    import numpy as np
    import concourse.bacc as bacc
    from concourse.bass_utils import run_bass_kernel_spmd

    nc = bacc.Bacc("TRN2", target_bir_lowering=False, num_devices=1)
    arrays, args = {}, []
    for name in _ORDER:
        a = np.ascontiguousarray(inputs[name])
        if name == "b_rel_bias":
            reach = (a.shape[2] - 1) // 2
            a = np.ascontiguousarray(a[0][:, np.clip(SEQ - 1 - np.arange(SPAN), -reach, reach) + reach])
        if a.ndim == 1:
            a = a.reshape(1, -1)
        arrays[f"in_{name}"] = a
        args.append(nc.dram_tensor(f"in_{name}", a.shape, mybir.dt.from_np(a.dtype), kind="ExternalInput").ap())
    consts = _constants()
    arrays["in_consts"] = consts
    args.append(nc.dram_tensor("in_consts", consts.shape, mybir.dt.float32, kind="ExternalInput").ap())
    args.append(nc.dram_tensor("out_0", (1, SEQ, D), mybir.dt.float32, kind="ExternalOutput").ap())
    trunk_kernel(nc, *args)
    r = run_bass_kernel_spmd(nc, [arrays], core_ids=[0])
    return r.results[0]["out_0"]
```
